# Optimizing a Trainium2 kernel written in Bass

```python
import math
import jax, jax.numpy as jnp
from jax import lax
import numpy as np

D_MODEL = 1024
BATCH = 1
SEQ = 512
DEPTH = 2

HEAD_DIM = 64
DIFF_HEADS = D_MODEL // (4 * HEAD_DIM)
FOX_HEADS = D_MODEL // (2 * HEAD_DIM)
DIFF_QK = DIFF_HEADS * 2 * HEAD_DIM
DIFF_V = DIFF_HEADS * 2 * HEAD_DIM
FOX_QK = FOX_HEADS * HEAD_DIM
FOX_V = FOX_HEADS * HEAD_DIM
ATTN_IN_SPLIT = (DIFF_QK, DIFF_QK, DIFF_V, FOX_QK, FOX_QK, FOX_V, FOX_HEADS)
ATTN_IN_WIDTH = sum(ATTN_IN_SPLIT)
ATTN_OUT_WIDTH = DIFF_V + FOX_V
Q_BLOCK = 128
FORGET_BIAS_INIT = 3.0
RNN_BLOCK_W = 128
RNN_WIDTH = (4 * D_MODEL // 3) // RNN_BLOCK_W * RNN_BLOCK_W
RNN_BLOCKS = RNN_WIDTH // RNN_BLOCK_W
CONV_WIDTH = 4
RG_C = 8.0
D_FF = 4 * D_MODEL
PLE_DIM = 256
N_ATTN_LAYERS = (DEPTH + 1) // 2
N_REC_LAYERS = DEPTH // 2
NORM_EPS = 1e-6
SUBLN_EPS = 1e-5


def rmsnorm(x, gain, eps=NORM_EPS):
    xf = x.astype(jnp.float32)
    y = xf * lax.rsqrt(jnp.mean(xf * xf, axis=-1, keepdims=True) + eps)
    return (y * gain.astype(jnp.float32)).astype(x.dtype)

def alibi_slopes(n_heads):
    return jnp.exp2(-8.0 * jnp.arange(1, n_heads + 1, dtype=jnp.float32) / n_heads)

def sweep_query_blocks(block_fn, batch, seq):
    out = lax.map(block_fn, jnp.arange(seq // Q_BLOCK))
    return jnp.moveaxis(out, 0, 1).reshape(batch, seq, out.shape[3], out.shape[4])

def differential_attention(q, k, v, lam):
    B, S, H, _, Dh = q.shape
    qf = q.astype(jnp.float32) * (Dh ** -0.5)
    kf = k.astype(jnp.float32)
    vf = v.astype(jnp.float32)
    slopes = alibi_slopes(H)
    kpos = jnp.arange(S)

    def block(i):
        qb = lax.dynamic_slice_in_dim(qf, i * Q_BLOCK, Q_BLOCK, axis=1)
        qpos = i * Q_BLOCK + jnp.arange(Q_BLOCK)
        s = jnp.einsum('bqhmd,bkhmd->bhmqk', qb, kf)
        dist = (qpos[:, None] - kpos[None, :]).astype(jnp.float32)
        s = s - (slopes[:, None, None] * dist)[None, :, None]
        causal = kpos[None, :] <= qpos[:, None]
        s = jnp.where(causal[None, None, None], s, -jnp.inf)
        pr = jax.nn.softmax(s, axis=-1)
        w = pr[:, :, 0] - lam * pr[:, :, 1]
        return jnp.einsum('bhqk,bkhe->bqhe', w, vf)

    return sweep_query_blocks(block, B, S)

def forgetting_attention(q, k, v, cum_log_f):
    B, S, H, Dh = q.shape
    qf = q.astype(jnp.float32) * (Dh ** -0.5)
    kf = k.astype(jnp.float32)
    vf = v.astype(jnp.float32)
    c_t = jnp.transpose(cum_log_f, (0, 2, 1))
    kpos = jnp.arange(S)

    def block(i):
        qb = lax.dynamic_slice_in_dim(qf, i * Q_BLOCK, Q_BLOCK, axis=1)
        cq = lax.dynamic_slice_in_dim(c_t, i * Q_BLOCK, Q_BLOCK, axis=2)
        qpos = i * Q_BLOCK + jnp.arange(Q_BLOCK)
        s = jnp.einsum('bqhd,bkhd->bhqk', qb, kf)
        s = s + (cq[..., :, None] - c_t[:, :, None, :])
        causal = kpos[None, :] <= qpos[:, None]
        s = jnp.where(causal[None, None], s, -jnp.inf)
        pr = jax.nn.softmax(s, axis=-1)
        return jnp.einsum('bhqk,bkhd->bqhd', pr, vf)

    return sweep_query_blocks(block, B, S)

def attention_mixer(hn, w_in, b_forget, w_out, lq1, lk1, lq2, lk2, subln, layer):
    B, S, _ = hn.shape
    z = hn @ w_in
    idx = [int(v) for v in np.cumsum(ATTN_IN_SPLIT)[:-1]]
    dq, dk, dv, fq, fk, fv, fz = jnp.split(z, idx, axis=-1)
    lam_init = 0.8 - 0.6 * math.exp(-0.3 * layer)
    lam = (jnp.exp(jnp.sum(lq1.astype(jnp.float32) * lk1.astype(jnp.float32)))
           - jnp.exp(jnp.sum(lq2.astype(jnp.float32) * lk2.astype(jnp.float32)))
           + lam_init)
    d_out = differential_attention(dq.reshape(B, S, DIFF_HEADS, 2, HEAD_DIM),
                                   dk.reshape(B, S, DIFF_HEADS, 2, HEAD_DIM),
                                   dv.reshape(B, S, DIFF_HEADS, 2 * HEAD_DIM), lam)
    d_out = rmsnorm(d_out, subln, eps=SUBLN_EPS) * (1.0 - lam_init)
    log_f = jax.nn.log_sigmoid(fz.astype(jnp.float32) + b_forget.astype(jnp.float32))
    cum_log_f = jnp.cumsum(log_f, axis=1)
    f_out = forgetting_attention(fq.reshape(B, S, FOX_HEADS, HEAD_DIM),
                                 fk.reshape(B, S, FOX_HEADS, HEAD_DIM),
                                 fv.reshape(B, S, FOX_HEADS, HEAD_DIM), cum_log_f)
    o = jnp.concatenate([d_out.reshape(B, S, DIFF_V), f_out.reshape(B, S, FOX_V)], axis=-1)
    return o.astype(hn.dtype) @ w_out

def _linear_recurrence_combine(earlier, later):
    a1, b1 = earlier
    a2, b2 = later
    return a1 * a2, a2 * b1 + b2

def recurrent_mixer(hn, w_in, conv_w, conv_b, wx, bx, wa, ba, a_param, w_out):
    B, S, _ = hn.shape
    gate_branch, xr = jnp.split(hn @ w_in, 2, axis=-1)
    y = jax.nn.gelu(gate_branch)
    xc = lax.conv_general_dilated(
        xr, conv_w.reshape(CONV_WIDTH, 1, RNN_WIDTH).astype(xr.dtype),
        window_strides=(1,), padding=[(CONV_WIDTH - 1, 0)],
        dimension_numbers=('NWC', 'WIO', 'NWC'),
        feature_group_count=RNN_WIDTH) + conv_b
    xb = xc.reshape(B, S, RNN_BLOCKS, RNN_BLOCK_W)
    gate_x = jax.nn.sigmoid(jnp.einsum('bsni,nij->bsnj', xb, wx).reshape(B, S, RNN_WIDTH) + bx)
    gate_a = jax.nn.sigmoid(jnp.einsum('bsni,nij->bsnj', xb, wa).reshape(B, S, RNN_WIDTH) + ba)
    log_a = RG_C * gate_a.astype(jnp.float32) * jax.nn.log_sigmoid(a_param.astype(jnp.float32))
    a = jnp.exp(log_a)
    mult = jnp.sqrt(-jnp.expm1(2.0 * log_a))
    mult = jnp.where((jnp.arange(S) == 0)[None, :, None], 1.0, mult)
    b = mult * gate_x.astype(jnp.float32) * xc.astype(jnp.float32)
    _, h = lax.associative_scan(_linear_recurrence_combine, (a, b), axis=1)
    return (h.astype(hn.dtype) * y) @ w_out

def first_inputs(seed: int = 0) -> dict:
    key = jax.random.key(seed)
    ks = iter(jax.random.split(key, 40))

    def nrm(shape, scale):
        return jax.random.normal(next(ks), shape, jnp.float32) * scale

    def gain(shape):
        return 1.0 + nrm(shape, 0.02)

    NA, NR = N_ATTN_LAYERS, N_REC_LAYERS
    u = jax.random.uniform(next(ks), (NR, RNN_WIDTH), jnp.float32, 0.9, 0.999)
    s = u ** (1.0 / RG_C)
    a_param = jnp.log(s) - jnp.log1p(-s)
    return {
        "x": nrm((BATCH, SEQ, D_MODEL), 1.0),
        "p": nrm((DEPTH, BATCH, SEQ, PLE_DIM), 1.0),
        "ln_mix_pre": gain((DEPTH, D_MODEL)),
        "ln_mix_post": gain((DEPTH, D_MODEL)),
        "ln_mlp_pre": gain((DEPTH, D_MODEL)),
        "ln_mlp_post": gain((DEPTH, D_MODEL)),
        "mlp_w_up": nrm((DEPTH, D_MODEL, D_FF), D_MODEL ** -0.5),
        "mlp_w_down": nrm((DEPTH, D_FF, D_MODEL), D_FF ** -0.5),
        "ple_w_proj": nrm((DEPTH, PLE_DIM, D_MODEL), PLE_DIM ** -0.5),
        "ple_norm": gain((DEPTH, D_MODEL)),
        "ple_w_gate": nrm((DEPTH, D_MODEL, D_MODEL), D_MODEL ** -0.5),
        "attn_w_in": nrm((NA, D_MODEL, ATTN_IN_WIDTH), D_MODEL ** -0.5),
        "attn_b_forget": FORGET_BIAS_INIT + nrm((NA, FOX_HEADS), 0.1),
        "attn_w_out": nrm((NA, ATTN_OUT_WIDTH, D_MODEL), ATTN_OUT_WIDTH ** -0.5),
        "diff_lambda_q1": nrm((NA, HEAD_DIM), 0.1),
        "diff_lambda_k1": nrm((NA, HEAD_DIM), 0.1),
        "diff_lambda_q2": nrm((NA, HEAD_DIM), 0.1),
        "diff_lambda_k2": nrm((NA, HEAD_DIM), 0.1),
        "diff_subln": gain((NA, 2 * HEAD_DIM)),
        "rec_w_in": nrm((NR, D_MODEL, 2 * RNN_WIDTH), D_MODEL ** -0.5),
        "rec_conv_w": nrm((NR, CONV_WIDTH, RNN_WIDTH), CONV_WIDTH ** -0.5),
        "rec_conv_b": nrm((NR, RNN_WIDTH), 0.01),
        "rec_wx": nrm((NR, RNN_BLOCKS, RNN_BLOCK_W, RNN_BLOCK_W), RNN_BLOCK_W ** -0.5),
        "rec_bx": nrm((NR, RNN_WIDTH), 0.01),
        "rec_wa": nrm((NR, RNN_BLOCKS, RNN_BLOCK_W, RNN_BLOCK_W), RNN_BLOCK_W ** -0.5),
        "rec_ba": nrm((NR, RNN_WIDTH), 0.01),
        "rec_a_param": a_param,
        "rec_w_out": nrm((NR, RNN_WIDTH, D_MODEL), RNN_WIDTH ** -0.5),
    }

def first_block(x, p, ln_mix_pre, ln_mix_post, ln_mlp_pre, ln_mlp_post, mlp_w_up, mlp_w_down,
              ple_w_proj, ple_norm, ple_w_gate, attn_w_in, attn_b_forget, attn_w_out,
              diff_lambda_q1, diff_lambda_k1, diff_lambda_q2, diff_lambda_k2, diff_subln,
              rec_w_in, rec_conv_w, rec_conv_b, rec_wx, rec_bx, rec_wa, rec_ba,
              rec_a_param, rec_w_out):
    h = x
    for layer in range(DEPTH):
        j = layer // 2
        hn = rmsnorm(h, ln_mix_pre[layer])
        if layer % 2 == 0:
            m = attention_mixer(hn, attn_w_in[j], attn_b_forget[j], attn_w_out[j],
                                diff_lambda_q1[j], diff_lambda_k1[j],
                                diff_lambda_q2[j], diff_lambda_k2[j], diff_subln[j], layer)
        else:
            m = recurrent_mixer(hn, rec_w_in[j], rec_conv_w[j], rec_conv_b[j], rec_wx[j],
                                rec_bx[j], rec_wa[j], rec_ba[j], rec_a_param[j], rec_w_out[j])
        h = h + rmsnorm(m, ln_mix_post[layer])
        u = rmsnorm(h, ln_mlp_pre[layer])
        f = jnp.square(jax.nn.relu(u @ mlp_w_up[layer])) @ mlp_w_down[layer]
        h = h + rmsnorm(f, ln_mlp_post[layer])
        e = rmsnorm(p[layer] @ ple_w_proj[layer], ple_norm[layer])
        h = h + e * jax.nn.sigmoid(h @ ple_w_gate[layer])
    return h


DEPTH_2 = 1

SSM_GROUP = 16
SSM_STATE = 64
SSM_WIDTH = D_MODEL // 2
SSM_GROUPS = SSM_WIDTH // SSM_GROUP
N_HEADS = D_MODEL // HEAD_DIM
N_KV = N_HEADS // 4
HPG = N_HEADS // N_KV
ATTN_WIDTH = N_HEADS * HEAD_DIM
KV_WIDTH = N_KV * HEAD_DIM
CMP_BLOCK = 32
CMP_STRIDE = 16
CMP_HIDDEN = 4 * HEAD_DIM
SLC_BLOCK = 64
SLC_TOPK = 16
WINDOW = 512
Q_CHUNK = 64
FORCED_SCORE = 1e4
IN_WIDTH = ATTN_WIDTH + 6 * KV_WIDTH + 3 * N_HEADS + SSM_WIDTH + 2 * D_MODEL
N_GROUPS = 4
EXP_PER_GROUP = 8
N_EXPERTS = N_GROUPS * EXP_PER_GROUP
TOPK_IN_GROUP = 2
D_EXPERT = D_MODEL // 4
MOE_BLOCK = 128
EPS = 1e-6
NEG = -1e30


def rms_norm(x, g):
    xf = x.astype(jnp.float32)
    y = xf * lax.rsqrt(jnp.mean(xf * xf, axis=-1, keepdims=True) + EPS)
    return (y * g.astype(jnp.float32)).astype(x.dtype)

def masked_softmax(s, mask):
    p = jax.nn.softmax(jnp.where(mask, s.astype(jnp.float32), NEG), axis=-1)
    return p * mask

def s5_mixer(u, lam_re, lam_im, log_dt, b_re, b_im, c_re, c_im, d_skip, w_glu):
    f32 = jnp.float32
    Bsz, L, _ = u.shape
    ug = u.astype(f32).reshape(Bsz, L, SSM_GROUPS, SSM_GROUP)
    dt = jnp.exp(log_dt.astype(f32))[:, None]
    lr, li = lam_re.astype(f32), lam_im.astype(f32)
    mag = jnp.exp(lr * dt)
    ab_re, ab_im = mag * jnp.cos(li * dt), mag * jnp.sin(li * dt)
    den = lr * lr + li * li
    nr = ab_re - 1.0
    cr = (nr * lr + ab_im * li) / den
    cim = (ab_im * lr - nr * li) / den
    br, bim = b_re.astype(f32), b_im.astype(f32)
    bb_re = cr[..., None] * br - cim[..., None] * bim
    bb_im = cr[..., None] * bim + cim[..., None] * br
    bu_re = jnp.einsum('blgh,gph->blgp', ug, bb_re)
    bu_im = jnp.einsum('blgh,gph->blgp', ug, bb_im)
    a_re = jnp.broadcast_to(ab_re, bu_re.shape)
    a_im = jnp.broadcast_to(ab_im, bu_im.shape)

    def combine(e1, e2):
        a1r, a1i, b1r, b1i = e1
        a2r, a2i, b2r, b2i = e2
        return (a2r * a1r - a2i * a1i, a2r * a1i + a2i * a1r,
                a2r * b1r - a2i * b1i + b2r, a2r * b1i + a2i * b1r + b2i)

    _, _, s_re, s_im = lax.associative_scan(combine, (a_re, a_im, bu_re, bu_im), axis=1)
    y = (jnp.einsum('blgp,ghp->blgh', s_re, c_re.astype(f32))
         - jnp.einsum('blgp,ghp->blgh', s_im, c_im.astype(f32))
         + d_skip.astype(f32) * ug)
    y = jax.nn.gelu(y.reshape(Bsz, L, SSM_WIDTH))
    y = y * jax.nn.sigmoid(y @ w_glu.astype(f32))
    return y.astype(u.dtype)

def compress_kv(kv, pos, w1, w2):
    Bsz, L, G, hd = kv.shape
    n_cmp = (L - CMP_BLOCK) // CMP_STRIDE + 1
    idx = jnp.arange(n_cmp)[:, None] * CMP_STRIDE + jnp.arange(CMP_BLOCK)[None, :]
    blocks = kv[:, idx] + pos[:, None, :]
    blocks = jnp.swapaxes(blocks, 2, 3).reshape(Bsz, n_cmp, G, CMP_BLOCK * hd)
    return jax.nn.gelu(blocks @ w1) @ w2

def nsa_attention(q, k_cmp, v_cmp, k_slc, v_slc, k_win, v_win, gates, cmp_pos, cmp_w1, cmp_w2):
    Bsz, L = q.shape[:2]
    n_cmp = (L - CMP_BLOCK) // CMP_STRIDE + 1
    n_slc = L // SLC_BLOCK
    n_sel = min(SLC_TOPK, n_slc)
    n_chunks = L // Q_CHUNK
    scale = HEAD_DIM ** -0.5
    kc = compress_kv(k_cmp, cmp_pos[0], cmp_w1[0], cmp_w2[0])
    vc = compress_kv(v_cmp, cmp_pos[1], cmp_w1[1], cmp_w2[1])
    cmp_end = jnp.arange(n_cmp) * CMP_STRIDE + CMP_BLOCK - 1
    c_start = jnp.arange(n_cmp)[:, None] * CMP_STRIDE
    s_start = jnp.arange(n_slc)[None, :] * SLC_BLOCK
    overlap = ((c_start < s_start + SLC_BLOCK) & (c_start + CMP_BLOCK > s_start)).astype(jnp.float32)
    ks_blk = jnp.moveaxis(k_slc.reshape(Bsz, n_slc, SLC_BLOCK, N_KV, HEAD_DIM), 3, 1)
    vs_blk = jnp.moveaxis(v_slc.reshape(Bsz, n_slc, SLC_BLOCK, N_KV, HEAD_DIM), 3, 1)
    kw = jnp.pad(k_win, ((0, 0), (WINDOW, 0), (0, 0), (0, 0)))
    vw = jnp.pad(v_win, ((0, 0), (WINDOW, 0), (0, 0), (0, 0)))
    bi = jnp.arange(Bsz)[:, None, None, None]
    gi = jnp.arange(N_KV)[None, :, None, None]
    blk = jnp.arange(n_slc)

    def chunk(args):
        c_idx, qc, gc = args
        t = c_idx * Q_CHUNK + jnp.arange(Q_CHUNK)
        s = jnp.einsum('bqghd,bngd->bqghn', qc, kc) * scale
        m = cmp_end[None, :] <= t[:, None]
        p_cmp = masked_softmax(s, m[None, :, None, None, :])
        o_cmp = jnp.einsum('bqghn,bngd->bqghd', p_cmp.astype(vc.dtype), vc)
        imp = jnp.einsum('bqghn,ns->bqgs', p_cmp, overlap)
        cur = t[:, None] // SLC_BLOCK
        forced = (blk[None, :] == 0) | (blk[None, :] == cur) | (blk[None, :] == cur - 1)
        future = blk[None, :] * SLC_BLOCK > t[:, None]
        imp = jnp.where(forced[None, :, None, :], FORCED_SCORE, imp)
        imp = jnp.where(future[None, :, None, :], -1.0, imp)
        _, sel = lax.top_k(imp, n_sel)
        sel = jnp.transpose(sel, (0, 2, 1, 3))
        ks = ks_blk[bi, gi, sel].reshape(Bsz, N_KV, Q_CHUNK, n_sel * SLC_BLOCK, HEAD_DIM)
        vs = vs_blk[bi, gi, sel].reshape(Bsz, N_KV, Q_CHUNK, n_sel * SLC_BLOCK, HEAD_DIM)
        kpos = (sel[..., None] * SLC_BLOCK + jnp.arange(SLC_BLOCK)).reshape(Bsz, N_KV, Q_CHUNK, n_sel * SLC_BLOCK)
        m = jnp.transpose(kpos <= t[None, None, :, None], (0, 2, 1, 3))[:, :, :, None, :]
        s = jnp.einsum('bqghd,bgqkd->bqghk', qc, ks) * scale
        p = masked_softmax(s, m)
        o_slc = jnp.einsum('bqghk,bgqkd->bqghd', p.astype(vs.dtype), vs)
        start = c_idx * Q_CHUNK
        kwc = lax.dynamic_slice_in_dim(kw, start, WINDOW + Q_CHUNK, axis=1)
        vwc = lax.dynamic_slice_in_dim(vw, start, WINDOW + Q_CHUNK, axis=1)
        wpos = start - WINDOW + jnp.arange(WINDOW + Q_CHUNK)
        d = t[:, None] - wpos[None, :]
        m = (d >= 0) & (d < WINDOW) & (wpos[None, :] >= 0)
        s = jnp.einsum('bqghd,bkgd->bqghk', qc, kwc) * scale
        p = masked_softmax(s, m[None, :, None, None, :])
        o_win = jnp.einsum('bqghk,bkgd->bqghd', p.astype(vwc.dtype), vwc)
        return (gc[:, :, 0, :, :, None] * o_cmp + gc[:, :, 1, :, :, None] * o_slc
                + gc[:, :, 2, :, :, None] * o_win)

    q_ch = jnp.moveaxis(q.reshape(Bsz, n_chunks, Q_CHUNK, N_KV, HPG, HEAD_DIM), 1, 0)
    g_ch = jnp.moveaxis(gates.reshape(Bsz, n_chunks, Q_CHUNK, 3, N_KV, HPG), 1, 0)
    o = lax.map(chunk, (jnp.arange(n_chunks), q_ch, g_ch))
    return jnp.moveaxis(o, 0, 1).reshape(Bsz, L, ATTN_WIDTH)

def token_mixer(h, w_in, ssm_lam_re, ssm_lam_im, ssm_log_dt, ssm_b_re, ssm_b_im, ssm_c_re, ssm_c_im,
                ssm_d, ssm_w_glu, ssm_w_o, nsa_cmp_pos, nsa_cmp_w1, nsa_cmp_w2, nsa_w_o, w_out):
    Bsz, L, _ = h.shape
    proj = h @ w_in
    o1 = ATTN_WIDTH
    o2 = o1 + 6 * KV_WIDTH
    o3 = o2 + 3 * N_HEADS
    o4 = o3 + SSM_WIDTH
    q, kv, nsa_g, u, merge_g = jnp.split(proj, [o1, o2, o3, o4], axis=-1)
    k_cmp, v_cmp, k_slc, v_slc, k_win, v_win = [t.reshape(Bsz, L, N_KV, HEAD_DIM) for t in jnp.split(kv, 6, axis=-1)]
    attn = nsa_attention(q.reshape(Bsz, L, N_KV, HPG, HEAD_DIM), k_cmp, v_cmp, k_slc, v_slc, k_win, v_win,
                         jax.nn.sigmoid(nsa_g).reshape(Bsz, L, 3, N_KV, HPG), nsa_cmp_pos, nsa_cmp_w1, nsa_cmp_w2)
    ssm = s5_mixer(u, ssm_lam_re, ssm_lam_im, ssm_log_dt, ssm_b_re, ssm_b_im, ssm_c_re, ssm_c_im, ssm_d, ssm_w_glu)
    g_attn, g_ssm = jnp.split(jax.nn.sigmoid(merge_g), 2, axis=-1)
    merged = g_attn * (attn @ nsa_w_o) + g_ssm * (ssm @ ssm_w_o)
    return merged @ w_out

def hier_moe(h, w_group, b_group, w_expert, b_expert, w_gate, w_up, w_down):
    Bsz, L, D = h.shape
    xt = h.reshape(-1, D)
    N = xt.shape[0]
    g_prob = jax.nn.softmax((xt @ w_group + b_group).astype(jnp.float32), axis=-1)
    g_p, g_idx = lax.top_k(g_prob, 1)
    e_logits = (xt @ w_expert + b_expert).astype(jnp.float32).reshape(N, N_GROUPS, EXP_PER_GROUP)
    e_logits = jnp.take_along_axis(e_logits, jnp.broadcast_to(g_idx[:, :, None], (N, 1, EXP_PER_GROUP)), axis=1)[:, 0]
    e_p, e_idx = lax.top_k(jax.nn.softmax(e_logits, axis=-1), TOPK_IN_GROUP)
    w = g_p * e_p / jnp.sum(e_p, axis=-1, keepdims=True)
    eid = g_idx * EXP_PER_GROUP + e_idx
    A = N * TOPK_IN_GROUP
    flat_e = eid.reshape(-1)
    flat_t = jnp.repeat(jnp.arange(N, dtype=jnp.int32), TOPK_IN_GROUP)
    flat_w = w.reshape(-1)
    order = jnp.argsort(flat_e)
    se = flat_e[order]
    counts = jnp.zeros(N_EXPERTS, jnp.int32).at[flat_e].add(1)
    starts = jnp.cumsum(counts) - counts
    pcounts = (counts + MOE_BLOCK - 1) // MOE_BLOCK * MOE_BLOCK
    pends = jnp.cumsum(pcounts)
    pstarts = pends - pcounts
    dest = pstarts[se] + jnp.arange(A) - starts[se]
    P = A + N_EXPERTS * MOE_BLOCK
    n_blk = P // MOE_BLOCK
    buf_t = jnp.zeros(P, jnp.int32).at[dest].set(flat_t[order])
    buf_w = jnp.zeros(P, jnp.float32).at[dest].set(flat_w[order])
    blk_e = jnp.minimum(jnp.searchsorted(pends, jnp.arange(n_blk) * MOE_BLOCK, side='right'), N_EXPERTS - 1)
    xs = xt[buf_t].reshape(n_blk, MOE_BLOCK, D)

    def expert_block(args):
        xb, e = args
        return (jax.nn.silu(xb @ w_gate[e]) * (xb @ w_up[e])) @ w_down[e]

    ys = lax.map(expert_block, (xs, blk_e)).reshape(P, D)
    out = jnp.zeros((N, D), jnp.float32).at[buf_t].add(ys.astype(jnp.float32) * buf_w[:, None])
    return out.astype(h.dtype).reshape(Bsz, L, D)

def second_inputs(seed: int = 0) -> dict:
    key = jax.random.key(seed)
    ks = jax.random.split(key, 32)
    f32 = jnp.float32

    def nrm(k, shape, s):
        return jax.random.normal(k, shape, f32) * s

    n_idx = jnp.arange(SSM_STATE, dtype=f32)
    return {
        'x': nrm(ks[0], (BATCH, SEQ, D_MODEL), 1.0),
        'c': nrm(ks[1], (BATCH, D_MODEL), 1.0),
        'ada_w': nrm(ks[2], (DEPTH_2, D_MODEL, 6 * D_MODEL), 0.5 * D_MODEL ** -0.5),
        'ada_b': nrm(ks[3], (DEPTH_2, 6 * D_MODEL), 0.01),
        'norm1_g': 1.0 + nrm(ks[4], (DEPTH_2, D_MODEL), 0.02),
        'w_in': nrm(ks[5], (DEPTH_2, D_MODEL, IN_WIDTH), D_MODEL ** -0.5),
        'ssm_lam_re': -0.5 + nrm(ks[6], (DEPTH_2, SSM_GROUPS, SSM_STATE), 0.01),
        'ssm_lam_im': math.pi * n_idx + nrm(ks[7], (DEPTH_2, SSM_GROUPS, SSM_STATE), 0.01),
        'ssm_log_dt': jax.random.uniform(ks[8], (DEPTH_2, SSM_GROUPS), f32, math.log(1e-3), math.log(1e-1)),
        'ssm_b_re': nrm(ks[9], (DEPTH_2, SSM_GROUPS, SSM_STATE, SSM_GROUP), (2 * SSM_GROUP) ** -0.5),
        'ssm_b_im': nrm(ks[10], (DEPTH_2, SSM_GROUPS, SSM_STATE, SSM_GROUP), (2 * SSM_GROUP) ** -0.5),
        'ssm_c_re': nrm(ks[11], (DEPTH_2, SSM_GROUPS, SSM_GROUP, SSM_STATE), SSM_STATE ** -0.5),
        'ssm_c_im': nrm(ks[12], (DEPTH_2, SSM_GROUPS, SSM_GROUP, SSM_STATE), SSM_STATE ** -0.5),
        'ssm_d': nrm(ks[13], (DEPTH_2, SSM_GROUPS, SSM_GROUP), 1.0),
        'ssm_w_glu': nrm(ks[14], (DEPTH_2, SSM_WIDTH, SSM_WIDTH), SSM_WIDTH ** -0.5),
        'ssm_w_o': nrm(ks[15], (DEPTH_2, SSM_WIDTH, D_MODEL), SSM_WIDTH ** -0.5),
        'nsa_cmp_pos': nrm(ks[16], (DEPTH_2, 2, CMP_BLOCK, HEAD_DIM), 0.02),
        'nsa_cmp_w1': nrm(ks[17], (DEPTH_2, 2, CMP_BLOCK * HEAD_DIM, CMP_HIDDEN), (CMP_BLOCK * HEAD_DIM) ** -0.5),
        'nsa_cmp_w2': nrm(ks[18], (DEPTH_2, 2, CMP_HIDDEN, HEAD_DIM), CMP_HIDDEN ** -0.5),
        'nsa_w_o': nrm(ks[19], (DEPTH_2, ATTN_WIDTH, D_MODEL), ATTN_WIDTH ** -0.5),
        'w_out': nrm(ks[20], (DEPTH_2, D_MODEL, D_MODEL), D_MODEL ** -0.5),
        'norm2_g': 1.0 + nrm(ks[21], (DEPTH_2, D_MODEL), 0.02),
        'moe_w_group': nrm(ks[22], (DEPTH_2, D_MODEL, N_GROUPS), D_MODEL ** -0.5),
        'moe_b_group': nrm(ks[23], (DEPTH_2, N_GROUPS), 0.01),
        'moe_w_expert': nrm(ks[24], (DEPTH_2, D_MODEL, N_EXPERTS), D_MODEL ** -0.5),
        'moe_b_expert': nrm(ks[25], (DEPTH_2, N_EXPERTS), 0.01),
        'moe_w_gate': nrm(ks[26], (DEPTH_2, N_EXPERTS, D_MODEL, D_EXPERT), D_MODEL ** -0.5),
        'moe_w_up': nrm(ks[27], (DEPTH_2, N_EXPERTS, D_MODEL, D_EXPERT), D_MODEL ** -0.5),
        'moe_w_down': nrm(ks[28], (DEPTH_2, N_EXPERTS, D_EXPERT, D_MODEL), D_EXPERT ** -0.5),
        'final_g': 1.0 + nrm(ks[29], (D_MODEL,), 0.02),
    }

def second_block(x, c, ada_w, ada_b, norm1_g, w_in, ssm_lam_re, ssm_lam_im, ssm_log_dt, ssm_b_re, ssm_b_im,
              ssm_c_re, ssm_c_im, ssm_d, ssm_w_glu, ssm_w_o, nsa_cmp_pos, nsa_cmp_w1, nsa_cmp_w2, nsa_w_o,
              w_out, norm2_g, moe_w_group, moe_b_group, moe_w_expert, moe_b_expert, moe_w_gate, moe_w_up,
              moe_w_down, final_g):
    cs = jax.nn.silu(c)
    for l in range(DEPTH_2):
        mod = cs @ ada_w[l] + ada_b[l]
        sh1, sc1, g1, sh2, sc2, g2 = jnp.split(mod[:, None, :], 6, axis=-1)
        h = rms_norm(x, norm1_g[l]) * (1.0 + sc1) + sh1
        x = x + g1 * token_mixer(h, w_in[l], ssm_lam_re[l], ssm_lam_im[l], ssm_log_dt[l], ssm_b_re[l],
                                 ssm_b_im[l], ssm_c_re[l], ssm_c_im[l], ssm_d[l], ssm_w_glu[l], ssm_w_o[l],
                                 nsa_cmp_pos[l], nsa_cmp_w1[l], nsa_cmp_w2[l], nsa_w_o[l], w_out[l])
        h = rms_norm(x, norm2_g[l]) * (1.0 + sc2) + sh2
        x = x + g2 * hier_moe(h, moe_w_group[l], moe_b_group[l], moe_w_expert[l], moe_b_expert[l],
                              moe_w_gate[l], moe_w_up[l], moe_w_down[l])
    return rms_norm(x, final_g)


def setup_inputs(seed=0):
    out = dict(first_inputs(seed))
    for name, value in second_inputs(seed + 1).items():
        if name != "x":
            out[name + "_2"] = value
    return out


def reference(
    x, p, ln_mix_pre, ln_mix_post, ln_mlp_pre, ln_mlp_post, mlp_w_up, mlp_w_down, ple_w_proj,
    ple_norm, ple_w_gate, attn_w_in, attn_b_forget, attn_w_out, diff_lambda_q1, diff_lambda_k1,
    diff_lambda_q2, diff_lambda_k2, diff_subln, rec_w_in, rec_conv_w, rec_conv_b, rec_wx,
    rec_bx, rec_wa, rec_ba, rec_a_param, rec_w_out, c_2, ada_w_2, ada_b_2, norm1_g_2, w_in_2,
    ssm_lam_re_2, ssm_lam_im_2, ssm_log_dt_2, ssm_b_re_2, ssm_b_im_2, ssm_c_re_2, ssm_c_im_2,
    ssm_d_2, ssm_w_glu_2, ssm_w_o_2, nsa_cmp_pos_2, nsa_cmp_w1_2, nsa_cmp_w2_2, nsa_w_o_2,
    w_out_2, norm2_g_2, moe_w_group_2, moe_b_group_2, moe_w_expert_2, moe_b_expert_2,
    moe_w_gate_2, moe_w_up_2, moe_w_down_2, final_g_2,
):
    x = first_block(
        x, p, ln_mix_pre, ln_mix_post, ln_mlp_pre, ln_mlp_post, mlp_w_up, mlp_w_down,
        ple_w_proj, ple_norm, ple_w_gate, attn_w_in, attn_b_forget, attn_w_out, diff_lambda_q1,
        diff_lambda_k1, diff_lambda_q2, diff_lambda_k2, diff_subln, rec_w_in, rec_conv_w,
        rec_conv_b, rec_wx, rec_bx, rec_wa, rec_ba, rec_a_param, rec_w_out,
    )
    return second_block(
        x, c_2, ada_w_2, ada_b_2, norm1_g_2, w_in_2, ssm_lam_re_2, ssm_lam_im_2, ssm_log_dt_2,
        ssm_b_re_2, ssm_b_im_2, ssm_c_re_2, ssm_c_im_2, ssm_d_2, ssm_w_glu_2, ssm_w_o_2,
        nsa_cmp_pos_2, nsa_cmp_w1_2, nsa_cmp_w2_2, nsa_w_o_2, w_out_2, norm2_g_2, moe_w_group_2,
        moe_b_group_2, moe_w_expert_2, moe_b_expert_2, moe_w_gate_2, moe_w_up_2, moe_w_down_2,
        final_g_2,
    )


_drawn_inputs = setup_inputs


def setup_inputs(seed=0):
    import zlib

    import numpy as np

    out = dict(_drawn_inputs(seed))
    spreads = {}
    factors = {'ln_mix_post': 2.949,
     'ln_mlp_pre': 3.106,
     'ln_mlp_post': 3.367,
     'ple_norm': 6.43,
     'attn_b_forget': 44.76,
     'diff_lambda_k2': 2.711,
     'diff_subln': 3.734,
     'rec_conv_b': 3.539,
     'rec_bx': 8.0,
     'rec_ba': 8.0,
     'ada_b_2': 8.0,
     'norm1_g_2': 8.0,
     'ssm_lam_re_2': 64.0,
     'ssm_lam_im_2': 64.0,
     'ssm_log_dt_2': 64.0,
     'ssm_b_re_2': 64.0,
     'ssm_b_im_2': 64.0,
     'ssm_c_re_2': 64.0,
     'ssm_c_im_2': 64.0,
     'ssm_w_glu_2': 7.04,
     'nsa_cmp_pos_2': 8.0,
     'nsa_cmp_w1_2': 4.662,
     'nsa_cmp_w2_2': 3.76,
     'norm2_g_2': 8.0,
     'moe_b_group_2': 8.0,
     'moe_b_expert_2': 36.123,
     'final_g_2': 7.774}
    for name, (base, spread) in spreads.items():
        noise = np.random.default_rng([zlib.crc32(name.encode()), seed]).standard_normal(out[name].shape)
        drawn = base * np.exp(spread * noise) if base else spread * noise
        out[name] = __import__('jax').numpy.asarray(drawn.astype(out[name].dtype))
    for name, factor in factors.items():
        out[name] = (out[name] * factor).astype(out[name].dtype)
    return out
```

```python
from contextlib import ExitStack
import math

import concourse.bass as bass
from concourse import mybir

ALU = mybir.AluOpType
ACT = mybir.ActivationFunctionType
AX = mybir.AxisListType.X
F32 = mybir.dt.float32
I32 = mybir.dt.int32

P = 128
T = 512
TT = T // P
D = 1024
KD = D // P
HD = 64
NSLOT = 8
NB = 4
NEG = -1e30
HUGE = 3.0e38
EPS = 1e-6
SUBLN_EPS = 1e-5
LAM_INIT = 0.8 - 0.6 * math.exp(-0.3 * 0)
DFF = 4096
RW = 1280
KR = RW // P
NE = 32
NG = 4
NEXP_G = NE // NG
NC = 32
CMP_STRIDE = 16
XT = T + CMP_STRIDE
NST = 16
TWO_PI = 2.0 * math.pi
LOG1P_TERMS = [1.0 / (2 * n + 1) for n in range(1, 10)]
STOP = "all"

VECTORS = [
    ("ln_mix_pre", 16), ("ln_mix_post", 16), ("ln_mlp_pre", 16), ("ln_mlp_post", 16), ("ple_norm", 16), ("ada_b_2", 48),
    ("norm1_g_2", 8), ("norm2_g_2", 8), ("final_g_2", 8), ("c_2", 8), ("rec_conv_w", 40), ("rec_conv_b", 10),
    ("rec_bx", 10), ("rec_ba", 10), ("rec_a_param", 10), ("ssm_d_2", 4),
    ("ssm_lam_re_2", 16), ("ssm_lam_im_2", 16), ("nsa_cmp_pos_2", 32),
]


def place_vectors():
    at, row = {}, 0
    for name, n in VECTORS:
        if row // P != (row + n - 1) // P:
            row = (row // P + 1) * P
        at[name] = row
        row += n
    return at, -(-row // P)


VROW, VTILES = place_vectors()

A_DQ, A_DK, A_DV, A_FQ, A_FK, A_FV, A_FZ = 0, 512, 1024, 1536, 2048, 2560, 3072
B_Q, B_KC, B_VC, B_KS, B_VS, B_KW, B_VW, B_GATE, B_U, B_MERGE = 0, 1024, 1280, 1536, 1792, 2048, 2304, 2560, 2608, 3120


def model_kernel(nc, t, out):
    ctx = ExitStack()
    with ctx:
        def sb(name, shape, dt=F32):
            return ctx.enter_context(nc.sbuf_tensor(name, shape, dt))

        sems = {}

        def sem(name):
            if name not in sems:
                sems[name] = ctx.enter_context(nc.semaphore(name))
            return sems[name]

        hT = sb("hT", [P, KD, T])
        xnT = sb("xnT", [P, KD, T])
        big = sb("big", [P, 40, T])
        mT = big[:, 32:40, :]
        ring = sb("ring", [P, NSLOT, 8 * P])
        ident = sb("ident", [P, P])
        ones = sb("ones", [P, P])
        tri = sb("tri", [P, P])
        rows = sb("rows", [P, VTILES, P])
        cols = sb("cols", [P, VTILES * P])
        rstd = sb("rstd", [P, T])
        rinv = sb("rinv", [P, T])
        selw = sb("selw", [P, 8, P])
        sel = selw[0:8, :, :]
        tmpA = sb("tmpA", [P, 2, T])
        tmpD = sb("tmpD", [P, 2, T])
        pbuf = sb("pbuf", [P, 3, T])
        ebuf = sb("ebuf", [P, 3, T])
        ptb = sb("ptb", [P, 2, T])
        nmax = sb("nmax", [P, 4])
        rsum = sb("rsum", [P, 4])
        small = sb("small", [P, 640])
        small2 = sb("small2", [P, 320])
        ot = sb("ot", [P, P])
        RCP = sb("rcp", [P, 4])
        rot = sb("rot", [P, T])
        OG = sb("og", [P, HD])
        banks = [ctx.enter_context(nc.psum_tensor(f"bank{i}", [P, T], F32)) for i in range(8)]
        stat = banks[4]
        wsc = nc.dram_tensor("expert_weights_scratch", (NE, T), F32, kind="Internal").ap()

        def col(name, k, n=1):
            c = VROW[name] + k
            return cols[:, c:c + n]

        def arena(a, n):
            return big[:, a:a + n, :]

        class Count:
            def __init__(self):
                self.tile = 0
                self.chunk = 0
                self.n = {}

            def step(self, name, k=1):
                self.n[name] = self.n.get(name, 0) + k
                return self.n[name]

        chunk_loaded = [sem(f"chunk_loaded{i}") for i in range(NSLOT)]
        chunk_used = sem("chunk_used")
        bank_free = [sem(f"bank_free{i}") for i in range(NB)]
        turned = sem("turned")

        def bank_of(n):
            return banks[n % NB]

        def free_bank(ins, n):
            ins.then_inc(bank_free[n % NB], 1)

        def evacuated(eng, n):
            eng.wait_ge(bank_free[n % NB], n // NB + 1)

        def chained(eng, name):
            s = sem(name)
            n = [0]

            def link(ins, wait=True):
                n[0] += 1
                ins.then_inc(s, 1)
                if wait:
                    eng.wait_ge(s, n[0])
                return n[0]
            link.sem, link.n = s, n
            return link

        def w_chunk(w, k0, kt, n0, m):
            return w[k0:k0 + kt * P, n0:n0 + m].rearrange("(k p) n -> p k n", p=P)

        def slot_view(c, kt, m):
            return ring[:, c % NSLOT, 0:kt * m].rearrange("p (k m) -> p k m", k=kt)

        W = {k: (v if k in ("mlp_w_up", "mlp_w_down", "ple_w_proj", "ple_w_gate", "p", "final_g_2") else v[0]) for k, v in t.items()}

        ALIBI = big[:, 24:28, :]
        V0 = big[:, 16:24, :].rearrange("p (a w) n -> p a w n", a=TT)
        FB = xnT
        FZ = [pbuf[0:8, 0, :], pbuf[0:8, 1, :], pbuf[0:8, 2, :], ebuf[0:8, 0, :], ebuf[0:8, 1, :]]
        CUM = ebuf[0:8, 2, :]
        LDOT, LEXP, NEGLAM = small[:, 386:388], small[:, 388:390], small[:, 390:391]
        EPSC, SEPSC = small[:, 391:392], small[:, 392:393]
        SS = small[:, 400:416]
        HBX, HBA, C4, NC4 = small[:, 416:426], small[:, 426:436], small[:, 436:446], small[:, 446:456]
        LPT = [small[:, 456 + 16 * j:472 + 16 * j] for j in range(5)]
        CIN = pbuf[:, :, :].rearrange("p a n -> p (a n)")[:, 0:2 * (T + 3)].rearrange("p (a n) -> p a n", a=2)
        GATEW = xnT[:, 0:5, :].rearrange("p a n -> p (a n)").rearrange("p (w i j) -> p w i j", w=2, i=KR)
        OTOK = mT.rearrange("p (a b) n -> p a (b n)", a=TT)
        PTOK = big[:, 16:18, :].rearrange("p a (b n) -> p (a b) n", b=2)

        QKV0 = ([A_FZ] + [A_DQ + P * j for j in range(4)] + [A_FQ + P * j for j in range(4)] + [A_DK + P * j for j in range(4)]
                + [A_FK + P * j for j in range(4)] + [A_DV + P * j for j in range(4)] + [A_FV + P * j for j in range(4)])
        NQK = 17


        MOD = small[:, 472:520]
        CS, GS1, GS2 = small[:, 520:528], small[:, 528:536], small[:, 536:544]
        CONE, CNEG = [small[:, P * j:P * (j + 1)].rearrange("p (q n) -> p q n", q=TT) for j in range(2)]
        GT = small2[:, 0:192].rearrange("p (q n) -> p q n", q=TT)
        PB = small2[:, 192:196]
        MASKB = small2[:, 200:232].rearrange("p (i g) -> p i g", i=4)
        MASKC = small2[:, 232:240]
        LOGDT = small2[:, 240:256]
        FLAT = big[:, :, :].rearrange("p a n -> p (a n)")
        XW = [FLAT[:, 28 * T + j * 4 * XT:28 * T + (j + 1) * 4 * XT].rearrange("p (g t) -> p g t", g=4) for j in range(2)]
        HID = big[:, 37, :].rearrange("p (v c n) -> p v c n", v=2, c=2)
        W2K = big[:, 38, 0:256].rearrange("p (c n) -> p c n", c=2)
        W2V = big[:, 38, 256:384].rearrange("p (c n) -> p c n", c=2)
        KCT = ot
        VBD = selw[:, :, :].rearrange("p a n -> p (a n)").rearrange("p (g n) -> p g n", g=4)
        BRAW, BB = ptb[:, 0, :].rearrange("p (c i h) -> p c i h", c=2, i=NST), ptb[:, 1, :].rearrange("p (c i h) -> p c i h", c=2, i=NST)
        CRAW = big[:, 39, :].rearrange("p (c u n) -> p c u n", c=2, u=4)
        POW = tmpA[:, 0, 0:9 * 32].rearrange("p (l c i) -> p l c i", l=9, c=2)

        def S16(j):
            return tmpA[:, 1, 16 * j:16 * j + 16]
        ROT_B = [x[:, :].rearrange("p (i n) -> p i n", i=NST) for x in (rstd, rinv)]
        ROT_A = [rot[:, 256 * j:256 * j + 256].rearrange("p (i n) -> p i n", i=NST) for j in range(2)]
        VTOK = [big[:, 28 + 2 * j:30 + 2 * j, :].rearrange("p a (b n) -> p (a b) n", b=2) for j in range(2)]
        CP = big[:, 4:8, :].rearrange("p q (h n) -> p q h n", h=16)
        WR = big[:, 30, 0:288].rearrange("p (k n) -> p k n", k=KD)
        BR = big[:, 31, 0:36]
        LG = pbuf[:, 0, 0:144].rearrange("p (q n) -> p q n", q=TT)
        WIN1 = [B_KC, B_KC + P, B_VC, B_VC + P, B_U, B_U + P, B_U + 2 * P, B_U + 3 * P, B_KS, B_KS + P, B_KW, B_KW + P]
        WIN1_TO = [24, 25, 26, 27, 0, 1, 2, 3, 16, 17, 18, 19]
        WIN2 = [B_VS, B_VS + P, B_VW, B_VW + P] + [B_Q + P * j for j in range(8)]
        WIN2_TO = [20, 21, 22, 23] + list(range(8, 16))
        N_WIN2 = len(WIN2)
        WIN1_TILE = [1 + KD + len(QKV0) + 16 + 2 * KD + (32 + 8 + 2 + 2 * KD) * 2 + 2 * KR + 2 * KR + KD + 1]

        def kv_slot(branch, h):
            g, b = h // 4, h % 2
            return (16 if g % 2 == b else 24) + 2 * branch + g // 2

        def loads2(sp, ct, chunk):
            def adaln(i):
                for j in range(NSLOT):
                    chunk(t["ada_w_2"][0, :, bass.ds(i * (NSLOT * P) + j * P, P)].rearrange("(k p) n -> p k n", p=P), KD, P, i, NSLOT)
            base = ct.chunk
            with sp.Fori(0, 6) as i:
                ct.chunk = base
                adaln(i)
            ct.chunk = base + 48
            for n0 in WIN1:
                chunk(w_chunk(W["w_in_2"], 0, KD, n0, P), KD, P)
            sp.wait_ge(sem("h_ready"), 48)
            w2 = W["nsa_cmp_w2_2"]
            for half in range(2):
                sp.dma_start(W2K[:, :, half * HD:(half + 1) * HD], w2[0].rearrange("(c p) d -> p c d", p=P)).then_inc(sem("w2_loaded"), 16)
            sp.dma_start(W2V, w2[1].rearrange("(c p) d -> p c d", p=P)).then_inc(sem("w2_loaded"), 16)
            for j, (bn, cn) in enumerate((("ssm_b_re_2", "ssm_c_re_2"), ("ssm_b_im_2", "ssm_c_im_2"))):
                sp.dma_start(BRAW[:, j], W[bn].rearrange("g p h -> (g p) h").rearrange("(i q) h -> q i h", q=P)).then_inc(sem("ssm_loaded"), 16)
                sp.dma_start(CRAW[:, j], W[cn].rearrange("g h p -> (g h) p").rearrange("(u q) n -> q u n", q=P)).then_inc(sem("ssm_loaded"), 16)
            ldt = W["ssm_log_dt_2"].rearrange("(i e) -> e i", e=2)
            for e in range(2):
                sp.dma_start(LOGDT[HD * e:HD * e + HD, :], ldt[e].partition_broadcast(HD), allow_slow_non_contiguous=True).then_inc(sem("ssm_loaded"), 16)
            for v in range(2):
                for c in range(2):
                    for half in range(2):
                        chunk(w_chunk(W["nsa_cmp_w1_2"][v], half * 8 * P, KD, c * P, P), KD, P)
            for n0 in WIN2:
                chunk(w_chunk(W["w_in_2"], 0, KD, n0, P), KD, P)
            chunk(w_chunk(W["w_in_2"], 0, KD, B_GATE, 48), KD, 48)
            for n in range(4):
                chunk(w_chunk(W["ssm_w_glu_2"], 0, 4, n * P, P), 4, P)
            for n in range(KD):
                chunk(w_chunk(W["w_in_2"], 0, KD, B_MERGE + n * P, P), KD, P)
                chunk(w_chunk(W["w_in_2"], 0, KD, B_MERGE + D + n * P, P), KD, P)
                chunk(w_chunk(W["nsa_w_o_2"], 0, KD, n * P, P), KD, P)
                chunk(w_chunk(W["ssm_w_o_2"], 0, 4, n * P, P), 4, P)
            sp.wait_ge(sem("att_out"), 192)
            sp.dma_start(WR[:, :, 0:4], W["moe_w_group_2"].rearrange("(k p) n -> p k n", p=P)).then_inc(sem("router_loaded"), 16)
            sp.dma_start(WR[:, :, 4:36], W["moe_w_expert_2"].rearrange("(k p) n -> p k n", p=P)).then_inc(sem("router_loaded"), 16)
            sp.dma_start(BR[:, 0:4], W["moe_b_group_2"].partition_broadcast(P)).then_inc(sem("router_loaded"), 16)
            sp.dma_start(BR[:, 4:36], W["moe_b_expert_2"].partition_broadcast(P)).then_inc(sem("router_loaded"), 16)
            for n in range(KD):
                chunk(w_chunk(W["w_out_2"], 0, KD, n * P, P), KD, P)
            base = ct.chunk
            with sp.Fori(0, NE // 4) as i:
                ct.chunk = base
                for q in range(4):
                    wg = [t[name][0, bass.ds(i * 4 + q, 1)].rearrange("e (k p) n -> p (e k) n", p=P) for name in ("moe_w_gate_2", "moe_w_up_2")]
                    wd = t["moe_w_down_2"][0, bass.ds(i * 4 + q, 1)].rearrange("e (k p) n -> p (e k) n", p=P)
                    for c in range(2):
                        for w in wg:
                            chunk(w[:, :, c * P:(c + 1) * P], KD, P, i, 24)
                    for c in range(2):
                        chunk(wd[:, :, c * 512:(c + 1) * 512], 2, 512, i, 24)

        def pool2(pool, link):
            G = nc.gpsimd
            pool.wait_ge(sem("h_ready"), 48)
            link(G.memset(CONE, 1.0))
            link(G.memset(CNEG, 0.0))
            for m, fill in ((CONE, 0.0), (CNEG, NEG)):
                G.affine_select(out=m, in_=m, compare_op=ALU.is_ge, fill=fill, base=-31, pattern=[[P, TT], [-CMP_STRIDE, NC]],
                                channel_multiplier=1).then_inc(sem("cmp_masks"), 1)
            link(G.memset(MASKB, 1.0))
            link(G.memset(MASKC, 1.0))
            link(G.affine_select(out=MASKB, in_=MASKB, compare_op=ALU.is_ge, fill=0.0, base=0, pattern=[[2 * HD, 4], [-HD, 8]], channel_multiplier=1))
            G.affine_select(out=MASKB, in_=MASKB, compare_op=ALU.is_ge, fill=0.0, base=HD - 1, pattern=[[-2 * HD, 4], [HD, 8]],
                            channel_multiplier=-1).then_inc(sem("ssm_masks"), 1)
            link(G.affine_select(out=MASKC, in_=MASKC, compare_op=ALU.is_ge, fill=0.0, base=0, pattern=[[-16, 8]], channel_multiplier=1))
            G.affine_select(out=MASKC, in_=MASKC, compare_op=ALU.is_ge, fill=0.0, base=15, pattern=[[16, 8]],
                            channel_multiplier=-1).then_inc(sem("ssm_masks"), 1)
            for v in range(2):
                for g in range(4):
                    evacuated(pool, WIN1_TILE[0] + 2 * v + g // 2)
                    pool.wait_ge(sem("window_pad"), 2)
                    src = big[HD * (g % 2):HD * (g % 2) + HD, 24 + 2 * v + g // 2, :]
                    pool.dma_start(XW[v][0:HD, g, 0:T], src).then_inc(sem("windows"), 16)
                    pool.dma_start(XW[v][HD:P, g, 0:T - 1], src[:, 1:T]).then_inc(sem("windows"), 16)
            pool.wait_ge(sem("rotations"), 1)
            for i in range(NST):
                if i >= 2:
                    pool.wait_ge(sem("s_ready"), 2 * (i - 1))
                er, ei, t1, t2 = [x.rearrange("p (a b) -> p a b", a=16) for x in (pbuf[:, i % 2, :], ebuf[:, i % 2, :], pbuf[:, 2, :], ebuf[:, 2, :])]
                ar, ai = [ROT_A[j][:, i, :].unsqueeze(2).broadcast_to([P, 16, 32]) for j in range(2)]
                br, bi = [ROT_B[j][:, i, :].unsqueeze(1).broadcast_to([P, 16, 32]) for j in range(2)]
                if i:
                    pool.wait_ge(sem("e_ready"), i)
                link(G.tensor_tensor(er, ar, br, ALU.mult), wait=False)
                link(G.tensor_tensor(t1, ai, bi, ALU.mult), wait=False)
                link(G.tensor_tensor(ei, ar, bi, ALU.mult), wait=False)
                link(G.tensor_tensor(t2, ai, br, ALU.mult))
                link(G.tensor_tensor(er, er, t1, ALU.subtract))
                G.tensor_tensor(ei, ei, t2, ALU.add).then_inc(sem("e_ready"), 1)
            pool.wait_ge(sem("y_step"), NST)
            for j in range(4):
                evacuated(pool, WIN1_TILE[0] + 8 + j)
                for half in range(2):
                    pool.dma_start(big[HD * half:HD * half + HD, 24 + j, :],
                                   big[HD * (1 - half):HD * (1 - half) + HD, 16 + j, :]).then_inc(sem("swapped"), 16)

        def pe2(pe, ct, open_tile, take_chunk, dense_tile, norm_sum, turn4, new_xn, attention):
            pe.wait_ge(sem("silu_c"), 1)
            bank = open_tile()
            c0 = ct.chunk
            with pe.Fori(0, 6) as i:
                ct.chunk = c0
                for j in range(NSLOT):
                    w = slot_view(take_chunk(i, NSLOT), KD, P)
                    for k in range(KD):
                        ins = pe.matmul(bank[:, bass.ds(i * NSLOT + j, 1)], w[:, k, :], CS[:, k:k + 1], start=(k == 0), stop=(k == KD - 1))
                    ins.then_inc(chunk_used, 1)
            ct.chunk = c0 + 48
            norm_sum(arena(20, KD))
            before = new_xn()
            for n in range(len(WIN1)):
                dense_tile([KD], lambda k: xnT[:, k, :], before=before if n == 0 else None)
            pe.wait_ge(sem("windows"), 16 * 16)
            for v in range(2):
                for c in range(2):
                    a, b = open_tile(), open_tile()
                    for half in range(2):
                        w = slot_view(take_chunk(), KD, P)
                        for q in range(KD):
                            jp = half * KD + q
                            x = XW[v][:, :, 2 * jp:2 * jp + CMP_STRIDE * (NC - 1) + 1:CMP_STRIDE]
                            pe.matmul(a[:, 0:P], w[:, q, :], x, start=(jp == 0), stop=(jp == 15))
                            ins = pe.matmul(b[:, 0:1], w[:, q, :], col("nsa_cmp_pos_2", 16 * v + jp), start=(jp == 0), stop=(jp == 15))
                        ins.then_inc(chunk_used, 1)
            pe.wait_ge(sem("hidden_cmp"), 4)
            pe.wait_ge(sem("w2_loaded"), 48)
            bank = open_tile()
            for c in range(2):
                ins = pe.matmul(bank[:, 0:P], W2K[:, c, :], HID[:, 0, c, :], start=(c == 0), stop=(c == 1))
            ins.then_inc(turned, 1)
            bank = open_tile()
            for hh in range(4):
                for g in range(4):
                    for c in range(2):
                        ins = pe.matmul(bank[hh * NC:(hh + 1) * NC, g * HD:(g + 1) * HD], HID[:, 1, c, g * NC:(g + 1) * NC], W2V[:, c, :],
                                        start=(c == 0), stop=(c == 1))
            ins.then_inc(turned, 1)
            for uu in range(4):
                for z in range(4):
                    pe.wait_ge(sem("z_built"), 4 * uu + z + 1)
                    turn4(lambda a: big[:, 28 + z, a * P:(a + 1) * P])
                tz = ct.tile
                for ii in range(4):
                    i = 4 * uu + ii
                    for z in range(2):
                        if ii == 0:
                            evacuated(pe, tz - 4 + z)
                        bank = open_tile()
                        pe.matmul(bank[:, :], big[:, 24 + z, ii * P:(ii + 1) * P], big[:, uu, :], start=True, stop=True).then_inc(turned, 1)
                    if i < N_WIN2:
                        dense_tile([KD], lambda k: xnT[:, k, :])
                    if ii == 0:
                        evacuated(pe, tz - 1)
                        evacuated(pe, tz - 2)
                        if uu:
                            pe.wait_ge(sem("y_taken"), uu)
                    for z in range(2):
                        pe.wait_ge(sem("s_ready"), 2 * i + z + 1)
                        ins = pe.matmul(banks[5][:, :], big[:, 26 + z, ii * P:(ii + 1) * P], big[:, 34 + z, :],
                                        start=(ii == 0 and z == 0), stop=(ii == 3 and z == 1))
                    ins.then_inc(sem("y_step"), 1)
            tg = ct.tile
            dense_tile([KD], lambda k: xnT[:, k, :], m=48)
            for j in range(4):
                turn4(lambda a: big[:, 20 + j, a * P:(a + 1) * P])
            evacuated(pe, tg)
            turn4(lambda a: ebuf[0:48, 0, a * P:(a + 1) * P], rows_=48)
            for n in range(4):
                dense_tile([4], lambda k: big[:, 4 + k, :], before=(lambda k: pe.wait_ge(sem("y_gelu"), k + 1)) if n == 0 else None)
            for q in range(TT):
                for odd in range(2):
                    bank = open_tile()
                    b = HD * odd
                    for j in range(8):
                        ins = pe.matmul(bank[:, j * NC:(j + 1) * NC], big[b:b + HD, 8 + j, q * P:(q + 1) * P],
                                        KCT[b:b + HD, (j // 2) * NC:(j // 2 + 1) * NC], start=True, stop=True)
                    ins.then_inc(turned, 1)
            for q in range(TT):
                pe.wait_ge(sem("cmp_probs"), q + 1)
                turn4(lambda a: big[:, 4 + q, a * P:(a + 1) * P])
                evacuated(pe, ct.tile - 1)
                for half in range(2):
                    bank = open_tile()
                    for g in range(2):
                        ins = pe.matmul(bank[:, g * 256:(g + 1) * 256], ptb[:, q % 2, (2 * half + g) * P:(2 * half + g + 1) * P],
                                        VBD[:, 2 * half + g, :], start=True, stop=True)
                    ins.then_inc(turned, 1)
            pe.wait_ge(sem("swapped"), 16 * 8)

            def qk2(u):
                m, qi = u // TT, u % TT
                branch, h = m // 16, m % 16
                b = HD * (h % 2)
                return (big[b:b + HD, 8 + h // 2, qi * P:(qi + 1) * P], big[b:b + HD, kv_slot(branch, h), :], qi)

            def v2(u, b):
                m = u // TT
                g = (m % 16) // 4
                return VTOK[m // 16][:, b, g * HD:(g + 1) * HD]
            attention(128, qk2, v2, lambda u: HD)
            pe.wait_ge(sem("o_added"), 128)
            ta = ct.tile
            for k in range(KD):
                turn4(lambda a: OTOK[:, a, k * P:(k + 1) * P])
            pe.wait_ge(sem("ssm_out"), 4)
            for n in range(KD):
                dense_tile([KD], lambda k: xnT[:, k, :])
                dense_tile([KD], lambda k: xnT[:, k, :])
                dense_tile([KD], lambda k: big[:, 8 + k, :], before=(lambda k: evacuated(pe, ta + k)) if n == 0 else None)
                dense_tile([4], lambda k: big[:, k, :])
            for n in range(KD):
                dense_tile([KD], lambda k: mT[:, k, :], before=(lambda k: pe.wait_ge(sem("merged"), k + 1)) if n == 0 else None)
            norm_sum(arena(16, KD))
            before = new_xn()
            before(KD - 1)
            pe.wait_ge(sem("router_loaded"), 64)
            bank = open_tile()
            for a in range(TT):
                for k in range(KD):
                    ins = pe.matmul(bank[:, a * 36:(a + 1) * 36], xnT[:, k, a * P:(a + 1) * P], WR[:, k, :], start=(k == 0), stop=(k == KD - 1))
            ins.then_inc(turned, 1)
            pe.wait_ge(sem("weights_ready"), 1)
            turn4(lambda a: WT[:, a, :], width=NE)
            t0, c0 = ct.tile, ct.chunk
            with pe.Fori(0, NE // 4) as i:
                ct.tile, ct.chunk = t0, c0
                for q in range(4):
                    hb = 28 + 2 * (q % 2)
                    for c in range(4):
                        dense_tile([KD], lambda k: xnT[:, k, :], i=i, tiles=48, chunks=24)
                    for c in (1, 3):
                        n = t0 + 12 * q + c
                        pe.wait_ge(bank_free[n % NB], n // NB + 1 + i * 12)
                    for c in range(2):
                        w = slot_view(take_chunk(i, 24), 2, 512)
                        for n in range(4):
                            bank = open_tile(i, 48)
                            for k in range(2):
                                ins = pe.matmul(bank[:, :], w[:, k, n * P:(n + 1) * P], big[:, hb + k, :], start=(k == 0), stop=(k == 1))
                            if n < 3:
                                ins.then_inc(sem("down_tiles"), 1)
                            else:
                                ins.then_inc(chunk_used, 1)
            ct.tile, ct.chunk = t0 + 384, c0 + 192
            norm_sum(arena(8, KD))
            before = new_xn()
            before(KD - 1)
            for a in range(TT):
                for half in range(2):
                    bank = banks[2 * a + half]
                    for k in range(4):
                        ins = pe.transpose(bank[:, k * P:(k + 1) * P], xnT[:, 4 * half + k, a * P:(a + 1) * P], ident[:, :])
                    ins.then_inc(turned, 1)

        def act2(act, ct, act_, take_tile, squares, square_tiles, root, attention):
            evacuated(act, 0)
            act_(CS, col("c_2", 0, KD), ACT.Silu).then_inc(sem("silu_c"), 1)
            squares(hT, arena(20, KD), first=lambda k: act.wait_ge(sem("h_ready"), 40 + k + 1))
            root()
            act.wait_ge(sem("ssm_loaded"), 96)
            act_(S16(0), LOGDT, ACT.Exp).then_inc(sem("dt_ready"), 1)
            act.wait_ge(sem("rates_ready"), 1)
            act_(S16(3), S16(1), ACT.Exp).then_inc(sem("ssm_functions"), 1)
            act.wait_ge(sem("angles_ready"), 1)
            act_(S16(6), S16(4), ACT.Sin).then_inc(sem("ssm_functions"), 1)
            act_(S16(7), S16(5), ACT.Sin).then_inc(sem("ssm_functions"), 1)
            ct.chunk, ct.tile = ct.chunk + 48 + 12, ct.tile + 1 + 12
            for v in range(2):
                for c in range(2):
                    ct.chunk += 2
                    act.wait_ge(chunk_used, ct.chunk)
                    evacuated(act, ct.tile + 1)
                    act_(HID[:, v, c, :], bank_of(ct.tile)[:, 0:P], ACT.Gelu_apprx_tanh, bias=PB[:, 2 * v + c:2 * v + c + 1]).then_inc(sem("hidden_cmp"), 1)
                    ct.tile += 2
            ct.tile += 2
            for uu in range(4):
                act.wait_ge(sem("y_taken"), uu + 1)
                act_(big[:, 4 + uu, :], tmpD[:, 0, :], ACT.Gelu_apprx_tanh).then_inc(sem("y_gelu"), 1)
            ct.chunk, ct.tile = ct.chunk + N_WIN2, ct.tile + 16 + 32 + N_WIN2
            b = take_tile(1)
            act.wait_ge(sem("s_ready"), 2 * NST)
            free_bank(act_(ebuf[0:48, 0, :], bank_of(b)[0:48, :], ACT.Sigmoid), b)
            ct.tile += 5
            for n in range(4):
                b = take_tile(1)
                if n >= 2:
                    act.wait_ge(sem("ssm_out"), n - 1)
                free_bank(act_(tmpD[:, n % 2, :], bank_of(b)[:, :], ACT.Sigmoid), b)
            for q in range(TT):
                act.wait_ge(sem("cmp_shifted"), q + 1)
                act_(big[:, 4 + q, :], big[:, 4 + q, :], ACT.Exp).then_inc(sem("cmp_exp"), 1)
            ct.tile += 8 + 12
            attention(128, True)
            ct.tile += KD
            for n in range(KD):
                for j in range(2):
                    b = take_tile(1)
                    if n:
                        act.wait_ge(sem("merged"), n)
                    free_bank(act_(tmpA[:, j, :], bank_of(b)[:, :], ACT.Sigmoid), b)
                ct.chunk, ct.tile = ct.chunk + 2, ct.tile + 2
            t0 = ct.tile
            squares(hT, arena(16, KD), first=lambda k: evacuated(act, t0 + k))
            ct.chunk, ct.tile = ct.chunk + KD, ct.tile + KD
            root()
            act.wait_ge(sem("router_shifted"), 1)
            act_(RT[0], RT[0], ACT.Exp).then_inc(sem("router_exp"), 1)
            act.wait_ge(sem("router_shifted"), 2)
            act_(RC[4], RC[3], ACT.Exp).then_inc(sem("router_exp"), 1)
            ct.tile += 2
            evacuated(act, ct.tile - 1)
            act.dma_start(wsc, WT32).then_inc(sem("weights_stored"), 16)
            act.wait_ge(sem("weights_stored"), 16)
            t0, c0 = ct.tile, ct.chunk
            with act.Fori(0, NE // 4) as i:
                for q in range(4):
                    for c in range(2):
                        act.wait_ge(chunk_used, c0 + 6 * q + 2 * c + 1 + i * 24)
                        if c == 0:
                            act.dma_start(big[:, 24 + q, :], wsc[bass.ds(i * 4 + q, 1), :].rearrange("a n -> (a n)").partition_broadcast(P)).then_inc(sem(f"weight_row{q}"), 16)
                        act.wait_ge(sem("silu_used"), 2 * q + c + 1 + i * 8)
                        free_bank(act_(tmpA[:, c, :], bank_of(t0 + 12 * q + 2 * c)[:, :], ACT.Silu), t0 + 12 * q + 2 * c)
            ct.tile, ct.chunk = t0 + 384, c0 + 192
            squares(hT, arena(8, KD), first=lambda k: act.wait_ge(sem("h_ready"), 48 + k + 1))
            root()

        RT = [pbuf[:, 1, 16 * j:16 * j + 16].rearrange("p (q n) -> p q n", q=TT) for j in range(6)]
        RC = [pbuf[:, 1, 128 + 4 * j:132 + 4 * j] for j in range(10)]
        RE = [pbuf[:, 2, P * j:P * (j + 1)].rearrange("p (q n) -> p q n", q=TT) for j in range(4)]
        RI = [ebuf[:, 2, P * j:P * (j + 1)] for j in range(2)]
        WT = ebuf[:, 1, 0:P].rearrange("p (q n) -> p q n", q=TT)
        WT32 = ebuf[0:NE, 0, :]

        def dve2(dve, ct, link, take_tile, take_turned, invert, apply_norm, add_to_h, copy_tiles, attention):
            V = nc.vector

            def tt(o, a, b, op):
                return link(V.tensor_tensor(o, a, b, op))

            def ts(o, a, s, op, s2=None, op2=None):
                if op2 is None:
                    return link(V.tensor_scalar(o, a, s, None, op))
                return link(V.tensor_scalar(o, a, s, s2, op, op2))

            def stt(o, a, s, b, op0, op1):
                return link(V.scalar_tensor_tensor(out=o, in0=a, scalar=s, in1=b, op0=op0, op1=op1))

            ADD, SUB, MUL, MIN, MAX, EQ = ALU.add, ALU.subtract, ALU.mult, ALU.min, ALU.max, ALU.is_equal
            ct.chunk += 48
            dve.wait_ge(chunk_used, ct.chunk)
            free_bank(V.tensor_tensor(MOD, bank_of(ct.tile)[:, 0:48], col("ada_b_2", 0, 48), ADD), ct.tile)
            evacuated(dve, ct.tile)
            ct.tile += 1
            stt(GS1, MOD[:, 8:16], 1.0, col("norm1_g_2", 0, KD), ADD, MUL)
            stt(GS2, MOD[:, 32:40], 1.0, col("norm2_g_2", 0, KD), ADD, MUL)
            ct.step("squares", KD)
            apply_norm(GS1, MOD[:, 0:8])
            for v in range(2):
                V.memset(XW[v][:, :, T - 1:XT], 0.0).then_inc(sem("window_pad"), 1)
            dve.wait_ge(sem("ssm_loaded"), 96)
            dve.wait_ge(sem("dt_ready"), 1)
            lr, li = col("ssm_lam_re_2", 0, NST), col("ssm_lam_im_2", 0, NST)
            dt, lrdt, th, mag, sa, ca, sin, cos, k = [S16(j) for j in range(9)]
            V.tensor_tensor(lrdt, lr, dt, MUL).then_inc(sem("rates_ready"), 1)
            tt(th, li, dt, MUL)
            ts(k, th, 1.0 / TWO_PI, MUL, 12582912.0, ADD)
            ts(k, k, -12582912.0, ADD)
            c1, c2 = 6.28125, 0.0019350051879882812
            c3 = TWO_PI - c1 - c2
            stt(th, k, -c1, th, MUL, ADD)
            stt(th, k, -c2, th, MUL, ADD)
            stt(th, k, -c3, th, MUL, ADD)
            lim = 3.1415925
            ts(sa, th, lim, MIN, -lim, MAX)
            ts(ca, th, math.pi / 2, ADD)
            ts(k, ca, math.pi, ALU.is_gt, -TWO_PI, MUL)
            tt(ca, ca, k, ADD)
            V.tensor_scalar(ca, ca, lim, -lim, MIN, MAX).then_inc(sem("angles_ready"), 1)
            dve.wait_ge(sem("ssm_functions"), 3)
            abr, abi, den, u1, u2, u3, cr, ci = [S16(9 + j) for j in range(8)]
            tt(abr, mag, cos, MUL)
            tt(abi, mag, sin, MUL)
            tt(den, lr, lr, MUL)
            tt(u1, li, li, MUL)
            tt(den, den, u1, ADD)
            link(V.reciprocal(den, den))
            ts(abr, abr, -1.0, ADD)
            tt(u1, abr, lr, MUL)
            tt(u2, abi, li, MUL)
            tt(u1, u1, u2, ADD)
            tt(cr, u1, den, MUL)
            tt(u1, abi, lr, MUL)
            tt(u2, abr, li, MUL)
            tt(u1, u1, u2, SUB)
            tt(ci, u1, den, MUL)

            def over_h(x):
                return x.unsqueeze(2).broadcast_to([P, NST, 16])
            tb = [tmpD[:, 1, 256 * j:256 * j + 256].rearrange("p (i h) -> p i h", i=NST) for j in range(2)]
            for o, a, b, op in ((0, 0, 1, SUB), (1, 1, 0, ADD)):
                tt(tb[0], BRAW[:, a], over_h(cr), MUL)
                tt(tb[1], BRAW[:, b], over_h(ci), MUL)
                tt(BB[:, o], tb[0], tb[1], op)
            link(V.tensor_copy(POW[:, 0, 0, :], cos))
            link(V.tensor_copy(POW[:, 0, 1, :], sin))
            for lv in range(8):
                tt(u1, POW[:, lv, 0, :], POW[:, lv, 0, :], MUL)
                tt(u2, POW[:, lv, 1, :], POW[:, lv, 1, :], MUL)
                tt(POW[:, lv + 1, 0, :], u1, u2, SUB)
                stt(POW[:, lv + 1, 1, :], POW[:, lv, 0, :], 2.0, POW[:, lv, 1, :], MUL, MUL)
            for (re, im), first, levels in ((ROT_B, 0, 5), (ROT_A, 5, 4)):
                link(V.memset(re[:, :, 0:1], 1.0))
                link(V.memset(im[:, :, 0:1], 0.0))
                for lv in range(levels):
                    m = 1 << lv
                    d1, d2 = [tmpD[:, 1, 256 * j:256 * j + 16 * m].rearrange("p (i n) -> p i n", i=NST) for j in range(2)]
                    pr, pi = [POW[:, first + lv, c, :].unsqueeze(2).broadcast_to([P, NST, m]) for c in range(2)]
                    tt(d1, re[:, :, 0:m], pr, MUL)
                    tt(d2, im[:, :, 0:m], pi, MUL)
                    tt(re[:, :, m:2 * m], d1, d2, SUB)
                    tt(d1, re[:, :, 0:m], pi, MUL)
                    tt(d2, im[:, :, 0:m], pr, MUL)
                    tt(im[:, :, m:2 * m], d1, d2, ADD)
            V.tensor_copy(u3, cos).then_inc(sem("rotations"), 1)

            for to in WIN1_TO:
                n = take_tile(1)
                free_bank(V.tensor_copy(big[:, to, :], bank_of(n)[:, :]), n)
            link(V.memset(VBD, 0.0))
            for v in range(2):
                for c in range(2):
                    ct.chunk += 2
                    dve.wait_ge(chunk_used, ct.chunk)
                    free_bank(V.tensor_copy(PB[:, 2 * v + c:2 * v + c + 1], bank_of(ct.tile + 1)[:, 0:1]), ct.tile + 1)
                    dve.wait_ge(sem("hidden_cmp"), 2 * v + c + 1)
                    free_bank(V.memset(small2[:, 196 + 2 * v + c:197 + 2 * v + c], 0.0), ct.tile)
                    ct.tile += 2
            n = take_turned()
            free_bank(V.tensor_copy(KCT[:, :], bank_of(n)[:, 0:P]), n)
            n = take_turned()
            for hh in range(4):
                ins = V.tensor_copy(VBD[hh * NC:(hh + 1) * NC, :, hh * HD:(hh + 1) * HD],
                                    bank_of(n)[hh * NC:(hh + 1) * NC, 0:256].rearrange("p (g d) -> p g d", g=4))
                if hh < 3:
                    link(ins, wait=False)
                else:
                    free_bank(ins, n)
            dve.wait_ge(sem("ssm_masks"), 2)
            zr, zi, sr, si, t1, t2, t3 = [big[:, j, :] for j in range(32, 39)]
            t4 = tmpD[:, 1, :]
            for uu in range(4):
                if uu:
                    dve.wait_ge(sem("s_ready"), 8 * uu)
                for z in range(4):
                    o = big[:, 28 + z, :]
                    if z < 2:
                        for ii in range(4):
                            ins = V.tensor_tensor(o[:, ii * P:(ii + 1) * P].rearrange("p (g h) -> p g h", g=8),
                                                  BB[:, z, 4 * uu + ii, :].unsqueeze(1).broadcast_to([P, 8, 16]),
                                                  MASKB[:, ii, :].unsqueeze(2).broadcast_to([P, 8, 16]), MUL)
                            if ii < 3:
                                link(ins, wait=False)
                    elif z == 2:
                        ins = V.tensor_tensor(o.rearrange("p (g n) -> p g n", g=8), CRAW[:, 0, uu, :].unsqueeze(1).broadcast_to([P, 8, HD]),
                                              MASKC.unsqueeze(2).broadcast_to([P, 8, HD]), MUL)
                    else:
                        tt(t1.rearrange("p (g n) -> p g n", g=8), CRAW[:, 1, uu, :].unsqueeze(1).broadcast_to([P, 8, HD]),
                           MASKC.unsqueeze(2).broadcast_to([P, 8, HD]), MUL)
                        ins = V.tensor_scalar(o, t1, -1.0, None, MUL)
                    ins.then_inc(sem("z_built"), 1)
                dve.wait_ge(sem("z_built"), 4 * uu + 4)
                if uu:
                    dve.wait_ge(sem("y_step"), 4 * uu)
                for z in range(4):
                    n = take_turned()
                    free_bank(V.tensor_copy(big[:, 24 + z, :], bank_of(n)[:, :]), n)
                for ii in range(4):
                    i = 4 * uu + ii
                    nr = take_turned()
                    ni = take_turned()
                    er, ei = pbuf[:, i % 2, :], ebuf[:, i % 2, :]
                    br, bi = bank_of(nr)[:, :], bank_of(ni)[:, :]
                    dve.wait_ge(sem("e_ready"), i + 1)
                    if i:
                        dve.wait_ge(sem("s_ready"), 2 * i)
                    link(V.tensor_tensor(t1, er, br, MUL), wait=False)
                    free_bank(V.tensor_tensor(t4, ei, br, MUL), nr)
                    link(V.tensor_tensor(t2, ei, bi, MUL), wait=False)
                    free_bank(V.tensor_tensor(t3, er, bi, MUL), ni)
                    dve.wait_ge(link.sem, link.n[0])
                    evacuated(dve, nr)
                    link(V.tensor_tensor(t1, t1, t2, ADD), wait=False)
                    evacuated(dve, ni)
                    tt(t3, t3, t4, SUB)
                    r = mag[:, i:i + 1].broadcast_to([P, T])
                    link(V.tensor_tensor_scan(zr, r, t1, 0.0, MUL, ADD), wait=False)
                    link(V.tensor_tensor_scan(zi, r, t3, 0.0, MUL, ADD))
                    link(V.tensor_tensor(t1, er, zr, MUL), wait=False)
                    link(V.tensor_tensor(t2, ei, zi, MUL), wait=False)
                    link(V.tensor_tensor(t3, er, zi, MUL), wait=False)
                    tt(t4, ei, zr, MUL)
                    if i:
                        dve.wait_ge(sem("y_step"), i)
                    V.tensor_tensor(sr, t1, t2, SUB).then_inc(sem("s_ready"), 1)
                    V.tensor_tensor(si, t3, t4, ADD).then_inc(sem("s_ready"), 1)
                    if i < N_WIN2:
                        n = take_tile(1)
                        if i >= 4:
                            free_bank(V.tensor_scalar(big[:, WIN2_TO[i], :], bank_of(n)[:, :], HD ** -0.5, None, MUL), n)
                        else:
                            free_bank(V.tensor_copy(big[:, WIN2_TO[i], :], bank_of(n)[:, :]), n)
                dve.wait_ge(sem("y_step"), 4 * uu + 4)
                if uu:
                    dve.wait_ge(sem("y_gelu"), uu)
                V.scalar_tensor_tensor(out=tmpD[:, 0, :], in0=big[:, uu, :], scalar=col("ssm_d_2", uu), in1=banks[5][:, :],
                                       op0=MUL, op1=ADD).then_inc(sem("y_taken"), 1)
            ct.chunk, ct.tile = ct.chunk + 1, ct.tile + 1
            for j in range(4):
                n = take_turned()
                free_bank(V.tensor_copy(VTOK[j // 2][:, :, (j % 2) * P:(j % 2 + 1) * P], bank_of(n)[:, :].rearrange("p (a n) -> p a n", a=TT)), n)
            n = take_turned()
            free_bank(V.tensor_copy(GT, bank_of(n)[:, 0:192].rearrange("p (a n) -> p a n", a=TT)), n)
            evacuated(dve, n)
            for n in range(4):
                ct.chunk, ct.tile = ct.chunk + 1, ct.tile + 1
                evacuated(dve, ct.tile - 1)
                V.tensor_tensor(big[:, n, :], big[:, 4 + n, :], tmpD[:, n % 2, :], MUL).then_inc(sem("ssm_out"), 1)
            dve.wait_ge(sem("cmp_masks"), 2)
            dve.wait_ge(sem("ssm_out"), 4)
            cmx = small2[:, 256:320].rearrange("p (q h) -> p q h", q=TT)
            for q in range(TT):
                for odd in range(2):
                    n = take_turned()
                    s = bank_of(n)[:, 0:8 * NC].rearrange("p (h n) -> p h n", h=8)
                    free_bank(V.tensor_tensor(CP[:, q, odd:16:2], s, CNEG[:, q, :].unsqueeze(1).broadcast_to([P, 8, NC]), ADD), n)
                    evacuated(dve, n)
                link(V.tensor_reduce(cmx[:, q, :], CP[:, q], AX, MAX))
                V.tensor_tensor(CP[:, q], CP[:, q], cmx[:, q, :].unsqueeze(2).broadcast_to([P, 16, NC]), SUB).then_inc(sem("cmp_shifted"), 1)
            for q in range(TT):
                dve.wait_ge(sem("cmp_exp"), q + 1)
                link(V.tensor_reduce(cmx[:, q, :], CP[:, q], AX, ADD))
                link(V.reciprocal(cmx[:, q, :], cmx[:, q, :]))
                tt(cmx[:, q, :], cmx[:, q, :], GT[:, q, 0:16], MUL)
                tt(CP[:, q], CP[:, q], CONE[:, q, :].unsqueeze(1).broadcast_to([P, 16, NC]), MUL)
                V.tensor_tensor(CP[:, q], CP[:, q], cmx[:, q, :].unsqueeze(2).broadcast_to([P, 16, NC]), MUL).then_inc(sem("cmp_probs"), 1)
            for q in range(TT):
                n = take_turned()
                free_bank(V.tensor_copy(ptb[:, q % 2, :], bank_of(n)[:, :]), n)
                for half in range(2):
                    n = take_turned()
                    free_bank(V.tensor_copy(OTOK[:, q, half * 512:(half + 1) * 512], bank_of(n)[:, :]), n)
            for k in range(4):
                evacuated(dve, ct.tile - 1 - k)

            def write2(u, bank, rcp, base):
                m, qi = u // TT, u % TT
                branch, h = m // 16, m % 16
                V.tensor_scalar(OG[:, 0:HD], bank[:, 0:HD], rcp, GT[:, qi, 16 + 16 * branch + h:17 + 16 * branch + h], MUL, MUL).then_inc(sem("att_out"), 1)
                dve.wait_ge(sem("att_out"), base + u + 1)
                o = OTOK[:, qi, h * HD:(h + 1) * HD]
                if m >= 16:
                    dve.wait_ge(sem("o_added"), u - 64 + 1)
                V.tensor_tensor(o, o, OG[:, 0:HD], ADD).then_inc(sem("o_added"), 1)
            attention(128, lambda u: None, write2)
            for k in range(KD):
                n = take_turned()
                free_bank(V.tensor_copy(big[:, 8 + k, :], bank_of(n)[:, :]), n)
            for n in range(KD):
                ct.chunk, ct.tile = ct.chunk + 2, ct.tile + 2
                if n:
                    dve.wait_ge(sem("merged"), n)
                for j in range(2):
                    b = take_tile(1)
                    evacuated(dve, b - 2)
                    free_bank(V.tensor_tensor(tmpD[:, j, :], bank_of(b)[:, :], tmpA[:, j, :], MUL), b)
                    evacuated(dve, b)
                V.tensor_tensor(mT[:, n, :], tmpD[:, 0, :], tmpD[:, 1, :], ADD).then_inc(sem("merged"), 1)
            for k in range(KD):
                b = take_tile(1)
                free_bank(V.scalar_tensor_tensor(out=hT[:, k, :], in0=bank_of(b)[:, :], scalar=MOD[:, 16 + k:17 + k], in1=hT[:, k, :],
                                                 op0=MUL, op1=ADD), b)
            for k in range(KD):
                evacuated(dve, ct.tile - KD + k)
            ct.step("squares", KD)
            apply_norm(GS2, MOD[:, 24:32])
            link(V.memset(RI[0][:, 0:1], 1000.0))
            for lv in range(5):
                ts(RI[0][:, 1 << lv:2 << lv], RI[0][:, 0:1 << lv], float(1 << lv), ADD)
            n = take_turned()
            free_bank(V.tensor_tensor(LG, bank_of(n)[:, 0:144].rearrange("p (q n) -> p q n", q=TT), BR.unsqueeze(1).broadcast_to([P, TT, 36]), ADD), n)
            evacuated(dve, n)

            def one_hot(logits, n, top, out_, scratch, c):
                link(V.tensor_reduce(top, logits, AX, MAX))
                tt(scratch, logits, top.unsqueeze(2).broadcast_to([P, TT, n]), EQ)
                stt(scratch, scratch, -1000.0, RI[0][:, 0:n].unsqueeze(1).broadcast_to([P, TT, n]), MUL, ADD)
                link(V.tensor_reduce(c, scratch, AX, MIN))
                tt(out_, scratch, c.unsqueeze(2).broadcast_to([P, TT, n]), EQ)
            gl, el = LG[:, :, 0:NG], LG[:, :, NG:NG + NE]
            gmax, gsum, m1, m2mm1, rr, c0_, m2, w1, w2, _ = RC
            one_hot(gl, NG, gmax, RT[1], RT[2], c0_)
            V.tensor_tensor(RT[0], gl, gmax.unsqueeze(2).broadcast_to([P, TT, NG]), SUB).then_inc(sem("router_shifted"), 1)
            ts(RT[3], RT[1], -NEG, MUL, NEG, ADD)
            for q in range(TT):
                tt(RE[0][:, q, :].rearrange("p (g e) -> p g e", g=NG), el[:, q, :].rearrange("p (g e) -> p g e", g=NG),
                   RT[3][:, q, :].unsqueeze(2).broadcast_to([P, NG, NEXP_G]), ADD)
            one_hot(RE[0], NE, m1, RE[1], RE[3], c0_)
            stt(RE[0], RE[1], NEG, RE[0], MUL, ADD)
            one_hot(RE[0], NE, m2, RE[2], RE[3], c0_)
            V.tensor_tensor(m2mm1, m2, m1, SUB).then_inc(sem("router_shifted"), 1)
            dve.wait_ge(sem("router_exp"), 2)
            link(V.tensor_reduce(gsum, RT[0], AX, ADD))
            ts(w1, rr, 1.0, ADD)
            tt(w1, w1, gsum, MUL)
            link(V.reciprocal(w1, w1))
            tt(w2, w1, rr, MUL)
            tt(RE[1], RE[1], w1.unsqueeze(2).broadcast_to([P, TT, NE]), MUL)
            tt(RE[2], RE[2], w2.unsqueeze(2).broadcast_to([P, TT, NE]), MUL)
            V.tensor_tensor(WT, RE[1], RE[2], ADD).then_inc(sem("weights_ready"), 1)
            n = take_turned()
            free_bank(V.tensor_copy(WT32, bank_of(n)[0:NE, :]), n)
            link(V.memset(mT, 0.0))
            for c in range(2):
                V.memset(tmpA[:, c, 0:1], 0.0).then_inc(sem("silu_used"), 1)
            t0, c0 = ct.tile, ct.chunk
            with dve.Fori(0, NE // 4) as i:
                for q in range(4):
                    for c in range(2):
                        g, u = t0 + 12 * q + 2 * c, t0 + 12 * q + 2 * c + 1
                        dve.wait_ge(bank_free[g % NB], g // NB + 1 + i * 12)
                        if c == 0:
                            dve.wait_ge(sem(f"weight_row{q}"), 16 + i * 16)
                        V.tensor_tensor(tmpD[:, c, :], tmpA[:, c, :], big[:, 24 + q, :], MUL).then_inc(sem("silu_used"), 1)
                        dve.wait_ge(sem("silu_used"), 2 * q + c + 3 + i * 8)
                        dve.wait_ge(chunk_used, c0 + 6 * q + 2 * c + 2 + i * 24)
                        free_bank(V.tensor_tensor(big[:, 28 + 2 * (q % 2) + c, :], bank_of(u)[:, :], tmpD[:, c, :], MUL), u)
                    for n in range(8):
                        b = t0 + 12 * q + 4 + n
                        if n % 4 < 3:
                            dve.wait_ge(sem("down_tiles"), 6 * q + 3 * (n // 4) + n % 4 + 1 + i * 24)
                        else:
                            dve.wait_ge(chunk_used, c0 + 6 * q + 4 + n // 4 + 1 + i * 24)
                        free_bank(V.tensor_tensor(mT[:, n, :], mT[:, n, :], bank_of(b)[:, :], ADD), b)
            ct.tile, ct.chunk = t0 + 384, c0 + 192
            for k in range(4):
                evacuated(dve, ct.tile - 1 - k)
            for k in range(KD):
                V.scalar_tensor_tensor(out=hT[:, k, :], in0=mT[:, k, :], scalar=MOD[:, 40 + k:41 + k], in1=hT[:, k, :],
                                       op0=MUL, op1=ADD).then_inc(sem("h_ready"), 1)
            dve.wait_ge(sem("h_ready"), ct.step("h", KD))
            ct.step("squares", KD)
            apply_norm(col("final_g_2", 0, KD))
            for j in range(2 * TT):
                dve.wait_ge(turned, ct.step("turned"))
                V.tensor_copy(OTOK[:, j // 2, (j % 2) * 512:(j % 2 + 1) * 512], banks[j][:, :]).then_inc(sem("result"), 1)

        def width0(n0):
            return 8 if n0 == A_FZ else P

        block = ctx.enter_context(nc.Block())

        @block.sync
        def _(sp):
            ct = Count()

            def chunk(src, kt, m, i=0, per=0):
                c = ct.chunk
                if c >= NSLOT:
                    sp.wait_ge(chunk_used, c - NSLOT + 1 + i * per)
                sp.dma_start(slot_view(c, kt, m), src).then_inc(chunk_loaded[c % NSLOT], 16)
                ct.chunk += 1

            def looped(n_iter, per, body):
                base = ct.chunk
                with sp.Fori(0, n_iter) as i:
                    ct.chunk = base
                    body(i)
                ct.chunk = base + n_iter * per

            sp.dma_start(OTOK, W["x"].rearrange("(a p) d -> p a d", p=P)).then_inc(sem("x_loaded"), 16)
            sp.wait_ge(sem("rows_cleared"), 1)
            for name, n in VECTORS:
                r = VROW[name]
                src = t[name]
                flat = {1: None, 2: "a b -> (a b)", 3: "a b c -> (a b c)", 4: "a b c d -> (a b c d)"}[len(src.shape)]
                if flat:
                    src = src.rearrange(flat)
                sp.dma_start(rows[r % P:r % P + n, r // P, :], src.rearrange("(r c) -> r c", c=P)).then_inc(sem("vectors_loaded"), 16)
            for j, name in enumerate(("diff_lambda_q1", "diff_lambda_k1", "diff_lambda_q2", "diff_lambda_k2")):
                sp.dma_start(small[:, 64 * j:64 * j + 64], W[name].partition_broadcast(P)).then_inc(sem("lambda_loaded"), 16)
            sp.dma_start(small[:, 256:384], W["diff_subln"].partition_broadcast(P)).then_inc(sem("lambda_loaded"), 16)
            sp.dma_start(small[0:8, 384:385], t["attn_b_forget"].rearrange("a b -> b a")).then_inc(sem("lambda_loaded"), 16)

            for n0 in QKV0:
                chunk(w_chunk(W["attn_w_in"], 0, KD, n0, width0(n0)), KD, width0(n0))
            for n in range(KD):
                chunk(w_chunk(W["attn_w_out"], 0, KD, n * P, P), KD, P)
            for layer in range(2):
                if layer == 1:
                    for n in list(range(KR, 2 * KR)) + list(range(KR)):
                        chunk(w_chunk(W["rec_w_in"], 0, KD, n * P, P), KD, P)
                    end_in = ct.chunk
                    for n in range(KD):
                        for half in range(2):
                            if (n, half) == (4, 0):
                                sp.wait_ge(chunk_used, end_in)
                                for w, name in enumerate(("rec_wx", "rec_wa")):
                                    sp.dma_start(GATEW[:, w], W[name].rearrange("n i j -> i n j")).then_inc(sem("gates_loaded"), 16)
                            chunk(w_chunk(W["rec_w_out"], half * 5 * P, 5, n * P, P), 5, P)

                def up(i):
                    for j in range(NSLOT):
                        chunk(t["mlp_w_up"][layer, :, bass.ds(i * (NSLOT * P) + j * P, P)].rearrange("(k p) n -> p k n", p=P), KD, P, i, NSLOT)
                looped(DFF // P // NSLOT, NSLOT, up)

                def down(i):
                    for j in range(4):
                        for q in range(4):
                            chunk(t["mlp_w_down"][layer, q * D:(q + 1) * D, bass.ds(i * (4 * P) + j * P, P)].rearrange("(k p) n -> p k n", p=P),
                                  KD, P, i, 16)
                looped(2, 16, down)
                end_down = ct.chunk
                for n in range(KD):
                    chunk(w_chunk(t["ple_w_proj"][layer], 0, 2, n * P, P), 2, P)
                sp.wait_ge(chunk_used, end_down)
                sp.dma_start(PTOK, t["p"][layer, 0].rearrange("(a p) d -> p a d", p=P)).then_inc(sem("p_loaded"), 16)
                for n in range(KD):
                    chunk(w_chunk(t["ple_w_gate"][layer], 0, KD, n * P, P), KD, P)
                if STOP == f"layer{layer}":
                    break
            if STOP == "all":
                loads2(sp, ct, chunk)
                sp.wait_ge(sem("result"), TT * 2)
                sp.dma_start(out.rearrange("a (b p) d -> p (a b) d", p=P), OTOK).then_inc(sem("stored"), 16)
            else:
                sp.wait_ge(sem("h_ready"), 24 * (int(STOP[-1]) + 1))
                sp.dma_start(out.rearrange("a (p q) d -> p (a q d)", p=P), hT[:, :, :].rearrange("p k n -> p (k n)")).then_inc(sem("stored"), 16)
            sp.wait_ge(sem("stored"), 16)

        @block.gpsimd
        def _(pool):
            link = chained(pool, "pool_chain")
            nc.gpsimd.memset(rows[:, :, :], 0.0).then_inc(sem("rows_cleared"), 1)
            link(nc.gpsimd.memset(ident[:, :], 0.0))
            nc.gpsimd.affine_select(out=ident[:, :], in_=ident[:, :], compare_op=ALU.not_equal, fill=1.0, base=0,
                                    pattern=[[-1, P]], channel_multiplier=1).then_inc(sem("constants"), 1)
            nc.gpsimd.memset(ones[:, :], 1.0).then_inc(sem("constants"), 1)
            link(nc.gpsimd.memset(tri[:, :], 0.0))
            nc.gpsimd.affine_select(out=tri[:, :], in_=tri[:, :], compare_op=ALU.is_ge, fill=NEG, base=0,
                                    pattern=[[-1, P]], channel_multiplier=1).then_inc(sem("constants"), 1)
            link(nc.gpsimd.memset(sel[:, :, :], 0.0))
            nc.gpsimd.affine_select(out=sel[:, :, :], in_=sel[:, :, :], compare_op=ALU.not_equal, fill=-1.0, base=0,
                                    pattern=[[-1, 8], [0, P]], channel_multiplier=1).then_inc(sem("constants"), 1)
            link(nc.gpsimd.iota(tmpD[:, 0, :].bitcast(I32), [[1, T]], base=-(T - P), channel_multiplier=-1))
            link(nc.gpsimd.tensor_copy(tmpD[:, 1, :], tmpD[:, 0, :].bitcast(I32)))
            for h in range(4):
                nc.gpsimd.tensor_scalar(ALIBI[:, h, :], tmpD[:, 1, :], 2.0 ** (-8.0 * (h + 1) / 4), None, ALU.mult).then_inc(sem("alibi"), 1)
            if STOP == "all":
                pool2(pool, link)

        @block.tensor
        def _(pe):
            ct = Count()
            pe.wait_ge(sem("constants"), 4)

            def open_tile(i=0, per=0):
                n = ct.tile
                if n // NB:
                    pe.wait_ge(bank_free[n % NB], n // NB + i * (per // NB))
                ct.tile += 1
                return bank_of(n)

            def take_chunk(i=0, per=0):
                c = ct.chunk
                pe.wait_ge(chunk_loaded[c % NSLOT], 16 * (c // NSLOT + 1) + i * (16 * (per // NSLOT)))
                ct.chunk += 1
                return c

            def dense_tile(kts, rhs, m=P, n=T, i=0, tiles=0, chunks=0, before=None):
                bank = open_tile(i, tiles)
                total, k = sum(kts), 0
                for kt in kts:
                    w = slot_view(take_chunk(i, chunks), kt, m)
                    for q in range(kt):
                        if before:
                            before(k)
                        ins = pe.matmul(bank[0:m, 0:n], w[:, q, :], rhs(k), start=(k == 0), stop=(k == total - 1))
                        k += 1
                    ins.then_inc(chunk_used, 1)

            def norm_sum(srcs):
                j = ct.step("norm")
                if j > 1:
                    pe.wait_ge(sem("stat_read"), j - 1)
                for k in range(KD):
                    pe.wait_ge(sem("squares"), KD * (j - 1) + k + 1)
                    ins = pe.matmul(stat[:, :], ones[:, :], srcs[:, k, :], start=(k == 0), stop=(k == KD - 1))
                ins.then_inc(sem("stat"), 1)

            def turn4(parts, rows_=P, width=P):
                bank = open_tile()
                for a in range(4):
                    ins = pe.transpose(bank[0:width, a * rows_:(a + 1) * rows_], parts(a), ident[0:rows_, 0:rows_])
                ins.then_inc(turned, 1)

            def new_xn():
                j = ct.step("xn")
                return lambda k: pe.wait_ge(sem("xn"), KD * (j - 1) + k + 1)

            def attention(n_units, qk, v_of, dv):
                base = ct.n.get("unit", 0)
                for b in range(NB):
                    evacuated(pe, ct.tile - 1 - (ct.tile - 1 - b) % NB)

                def scores(u):
                    if u >= 3:
                        pe.wait_ge(sem("att_exp"), base + u - 2)
                    q, k, qi = qk(u)
                    s = banks[5 + u % 3]
                    n = (qi + 1) * P
                    pe.matmul(s[:, 0:n], q, k[:, 0:n], start=True, stop=False, skip_group_check=True)
                    pe.matmul(s[:, n - P:n], ident[:, :], tri[:, :], start=False, stop=True, skip_group_check=True).then_inc(sem("att_scores"), 1)

                def wait_copy(u):
                    pe.wait_ge(sem(f"att_copied{u % 2}"), base // 2 + u // 2 + 1)

                def turn(u):
                    pe.wait_ge(sem("att_exp"), base + u + 1)
                    if u >= 2:
                        wait_copy(u - 2)
                    for b in range(qk(u)[2] + 1):
                        ins = pe.transpose(banks[u % 2][:, b * P:(b + 1) * P], ebuf[:, u % 3, b * P:(b + 1) * P], ident[:, :])
                    ins.then_inc(sem("att_turned"), 1)

                def values(u):
                    wait_copy(u)
                    if u >= 2:
                        pe.wait_ge(sem("att_out"), base + u - 1)
                    qi = qk(u)[2]
                    for b in range(qi + 1):
                        ins = pe.matmul(banks[2 + u % 2][:, 0:dv(u)], ptb[:, u % 2, b * P:(b + 1) * P], v_of(u, b),
                                        start=(b == 0), stop=(b == qi))
                    ins.then_inc(sem("att_values"), 1)

                for s in range(n_units + 3):
                    if s < n_units:
                        scores(s)
                    if 2 <= s < n_units + 2:
                        turn(s - 2)
                    if s >= 3:
                        values(s - 3)
                pe.wait_ge(sem("att_out"), base + n_units)
                ct.n["unit"] = base + n_units

            pe.wait_ge(sem("vectors_loaded"), 16 * len(VECTORS))
            bank = open_tile()
            for a in range(VTILES):
                ins = pe.transpose(bank[:, a * P:(a + 1) * P], rows[:, a, :], ident[:, :])
            ins.then_inc(turned, 1)
            pe.wait_ge(sem("x_loaded"), 16)
            for k in range(KD):
                turn4(lambda a: OTOK[:, a, k * P:(k + 1) * P])
            norm_sum(arena(0, KD))

            before = new_xn()
            tile0 = ct.tile
            for j, n0 in enumerate(QKV0):
                dense_tile([KD], lambda k: xnT[:, k, :], m=width0(n0), before=before if j == 0 else None)
            for j in range(8):
                evacuated(pe, tile0 + NQK + j)
                turn4(lambda a: mT[:, j, a * P:(a + 1) * P])
            pe.wait_ge(sem("log_forget"), 1)
            for h in range(8):
                bank = open_tile()
                pe.matmul(bank[:, :], sel[:, h, :], CUM, start=True, stop=True).then_inc(turned, 1)

            def qk0(u):
                m, qi = u // TT, u % TT
                tile, b = m // 2, HD * (m % 2)
                return (big[b:b + HD, tile, qi * P:(qi + 1) * P], big[b:b + HD, 8 + tile, :], qi)

            def v0(u, b):
                m = u // TT
                if m < 8:
                    return V0[:, b, 0, (m // 2) * P:(m // 2 + 1) * P]
                return V0[:, b, 1, (m - 8) * HD:(m - 7) * HD]
            attention(64, qk0, v0, lambda u: P if u < 32 else HD)
            pe.wait_ge(sem("subln_done"), TT)
            tile0 = ct.tile
            for k in range(KD):
                turn4(lambda a: OTOK[:, a, k * P:(k + 1) * P])
            for n in range(KD):
                dense_tile([KD], lambda k: xnT[:, k, :], before=(lambda k: evacuated(pe, tile0 + k)) if n == 0 else None)
            norm_sum(arena(0, KD))

            for layer in range(2):
                if layer == 1:
                    norm_sum(arena(0, KD))
                    before = new_xn()
                    for n in range(2 * KR):
                        dense_tile([KD], lambda k: xnT[:, k, :], before=before if n == 0 else None)
                    pe.wait_ge(sem("gates_loaded"), 32)
                    for i in range(KR):
                        pe.wait_ge(sem("conv_out"), i + 1)
                        for g in range(2):
                            bank = open_tile()
                            pe.matmul(bank[:, :], GATEW[:, g, i, :], big[:, i, :], start=True, stop=True).then_inc(turned, 1)
                    for n in range(KD):
                        dense_tile([5, 5], lambda k: big[:, k, :], before=(lambda k: pe.wait_ge(sem("rec_out"), k + 1)) if n == 0 else None)
                    norm_sum(arena(10, KD))
                norm_sum(arena(10, KD))
                before = new_xn()
                before(KD - 1)
                tile0, chunk0 = ct.tile, ct.chunk
                with pe.Fori(0, 4) as i:
                    ct.tile, ct.chunk = tile0, chunk0
                    for j in range(8):
                        dense_tile([KD], lambda k: xnT[:, k, :], i=i, tiles=8, chunks=8)
                ct.tile, ct.chunk = tile0 + 32, chunk0 + 32
                pe.wait_ge(sem("hidden"), 32 * (layer + 1))
                tile0, chunk0 = ct.tile, ct.chunk
                with pe.Fori(0, 2) as i:
                    ct.tile, ct.chunk = tile0, chunk0
                    for j in range(4):
                        dense_tile([KD] * 4, lambda k: big[:, k, :], i=i, tiles=4, chunks=16)
                ct.tile, ct.chunk = tile0 + 8, chunk0 + 32
                norm_sum(xnT)
                pe.wait_ge(sem("p_loaded"), 16 * (layer + 1))
                tile0 = ct.tile
                for k in range(2):
                    turn4(lambda a: PTOK[:, a, k * P:(k + 1) * P])
                for n in range(KD):
                    dense_tile([2], lambda k: big[:, 18 + k, :], before=(lambda k: evacuated(pe, tile0 + k)) if n == 0 else None)
                norm_sum(arena(8, KD))
                pe.wait_ge(sem("h_ready"), 24 * layer + 16)
                for n in range(KD):
                    dense_tile([KD], lambda k: hT[:, k, :])
                if STOP == f"layer{layer}":
                    break
            if STOP == "all":
                pe2(pe, ct, open_tile, take_chunk, dense_tile, norm_sum, turn4, new_xn, attention)

        @block.scalar
        def _(act):
            ct = Count()

            def act_(out_, in_, func, **kw):
                return nc.scalar.activation(out_, in_, func, **kw)

            def take_tile(chunks):
                ct.chunk += chunks
                act.wait_ge(chunk_used, ct.chunk)
                ct.tile += 1
                return ct.tile - 1

            def squares(srcs, dst, first):
                for k in range(KD):
                    first(k)
                    act_(dst[:, k, :], srcs[:, k, :], ACT.Square).then_inc(sem("squares"), 1)
                ct.step("squares", KD)

            def square_tiles(dst, chunks_per_tile):
                for k in range(KD):
                    n = take_tile(chunks_per_tile)
                    act_(dst[:, k, :], bank_of(n)[:, :], ACT.Square).then_inc(sem("squares"), 1)
                ct.step("squares", KD)

            def root():
                j = ct.step("norm")
                act.wait_ge(sem("stat"), j)
                if j > 1:
                    act.wait_ge(sem("rinv"), j - 1)
                act_(rstd[:, :], stat[:, :], ACT.Sqrt, scale=1.0 / D, bias=EPSC).then_inc(sem("stat_read"), 1)

            def attention(n_units, from_psum):
                base = ct.n.get("unit", 0)

                def expo(u):
                    act.wait_ge(sem("att_max"), base + u + 1)
                    if u >= 3:
                        act.wait_ge(sem("att_turned"), base + u - 2)
                    if u >= 4:
                        act.wait_ge(sem("att_out"), base + u - 3)
                    n = (u % TT + 1) * P
                    src = banks[5 + u % 3] if from_psum else pbuf[:, u % 3]
                    act_(ebuf[:, u % 3, 0:n], src[:, 0:n], ACT.Exp, scale=1.0 if from_psum else -1.0,
                         bias=nmax[:, u % 4:u % 4 + 1], accum_out=rsum[:, u % 4:u % 4 + 1]).then_inc(sem("att_exp"), 1)

                def copy(u):
                    act.wait_ge(sem("att_turned"), base + u + 1)
                    if u >= 2:
                        act.wait_ge(sem("att_values"), base + u - 1)
                    n = (u % TT + 1) * P
                    act_(ptb[:, u % 2, 0:n], banks[u % 2][:, 0:n], ACT.Copy).then_inc(sem("att_copied1"), 1)

                for s in range(n_units + 2):
                    if s < n_units:
                        expo(s)
                    if s >= 2 and s % 2 == 1:
                        copy(s - 2)
                ct.n["unit"] = base + n_units

            act.wait_ge(sem("lambda_dots"), 1)
            act_(LEXP, LDOT, ACT.Exp).then_inc(sem("lambda_exp"), 1)
            act.wait_ge(sem("a_param_in"), 1)
            act_(LPT[1][:, 0:KR], LPT[0][:, 0:KR], ACT.Exp, scale=-1.0).then_inc(sem("a_param_exp"), 1)
            ct.tile = 1 + KD
            squares(hT, arena(0, KD), first=lambda k: evacuated(act, 1 + k))
            root()
            act.wait_ge(sem("forget_in"), 1)
            act_(FZ[2], FZ[1], ACT.Exp, scale=-1.0).then_inc(sem("forget_exp"), 1)
            ct.chunk, ct.tile = len(QKV0), ct.tile + len(QKV0) + 16
            attention(64, False)
            act.wait_ge(sem("subln_sums"), 1)
            act_(SS, SS, ACT.Sqrt, scale=1.0 / P, bias=SEPSC).then_inc(sem("subln_root"), 1)
            ct.tile += KD
            square_tiles(arena(0, KD), 1)
            root()
            for layer in range(2):
                if layer == 1:
                    squares(hT, arena(0, KD), first=lambda k: act.wait_ge(sem("h_ready"), 16 + k + 1))
                    root()
                    ct.chunk, ct.tile = ct.chunk + KR, ct.tile + KR
                    for n in range(KR):
                        b = take_tile(1)
                        free_bank(act_(big[:, 10 + n, :], bank_of(b)[:, :], ACT.Gelu_apprx_tanh), b)
                    act.wait_ge(sem("c4_ready"), 1)
                    base_turned = 1 + KD + 8 + 8 + KD + 2
                    for i in range(KR):
                        act.wait_ge(turned, base_turned + 2 * i + 1)
                        if i >= 2:
                            act.wait_ge(sem("gate_x_used"), i - 1)
                        free_bank(act_(tmpA[:, i % 2, :], bank_of(ct.tile)[:, :], ACT.Tanh, scale=0.5, bias=HBX[:, i:i + 1]), ct.tile)
                        ct.tile += 1
                        act.wait_ge(turned, base_turned + 2 * i + 2)
                        if i >= 1:
                            act.wait_ge(sem("gate_a_read"), 2 * i)
                        free_bank(act_(rstd[:, :], bank_of(ct.tile)[:, :], ACT.Tanh, scale=0.5, bias=HBA[:, i:i + 1]), ct.tile)
                        evacuated(act, ct.tile)
                        ct.tile += 1
                        act_(big[:, 20 + i, :], rstd[:, :], ACT.Exp, scale=C4[:, i:i + 1], bias=C4[:, i:i + 1]).then_inc(sem("gate_a_read"), 1)
                        act_(big[:, 30 + i, :], rstd[:, :], ACT.Tanh, scale=NC4[:, i:i + 1], bias=NC4[:, i:i + 1]).then_inc(sem("gate_a_read"), 1)
                    for i in range(KR):
                        act.wait_ge(sem("one_minus_a2"), i + 1)
                        act_(big[:, 30 + i, :], big[:, 30 + i, :], ACT.Sqrt).then_inc(sem("mult_ready"), 1)
                    square_tiles(arena(10, KD), 2)
                    root()
                squares(hT, arena(10, KD), first=lambda k: act.wait_ge(sem("h_ready"), 24 * layer + k + 1))
                root()
                ct.chunk, ct.tile = ct.chunk + 32, ct.tile + 32
                c0, t0 = ct.chunk, ct.tile
                with act.Fori(0, 2) as i:
                    for j in range(4):
                        act.wait_ge(chunk_used, c0 + 4 * (j + 1) + i * 16)
                        act_(xnT[:, bass.ds(i * 4 + j, 1), :], bank_of(t0 + j)[:, :], ACT.Square).then_inc(sem("squares"), 1)
                ct.chunk, ct.tile = c0 + 32, t0 + 8
                ct.step("squares", KD)
                root()
                ct.tile += 2
                square_tiles(arena(8, KD), 1)
                root()
                for k in range(KD):
                    n = take_tile(1)
                    g = ct.step("gated")
                    if g > 2:
                        act.wait_ge(sem("gated"), g - 2)
                    free_bank(act_(tmpA[:, k % 2, :], bank_of(n)[:, :], ACT.Sigmoid), n)
                if STOP == f"layer{layer}":
                    break
            if STOP == "all":
                act2(act, ct, act_, take_tile, squares, square_tiles, root, attention)

        @block.vector
        def _(dve):
            ct = Count()
            link = chained(dve, "dve_chain")
            V = nc.vector

            def take_tile(chunks):
                ct.chunk += chunks
                dve.wait_ge(chunk_used, ct.chunk)
                ct.tile += 1
                return ct.tile - 1

            def take_turned(k=1):
                dve.wait_ge(turned, ct.step("turned"))
                ct.tile += 1
                return ct.tile - 1

            def invert():
                j = ct.step("norm")
                dve.wait_ge(sem("stat_read"), j)
                V.reciprocal(rinv[:, :], rstd[:, :]).then_inc(sem("rinv"), 1)
                dve.wait_ge(sem("rinv"), j)

            def apply_norm(gain, shift=None):
                invert()
                for k in range(KD):
                    ins = V.scalar_tensor_tensor(out=xnT[:, k, :], in0=hT[:, k, :], scalar=gain[:, k:k + 1], in1=rinv[:, :],
                                                 op0=ALU.mult, op1=ALU.mult)
                    if shift is not None:
                        link(ins)
                        ins = V.tensor_scalar(xnT[:, k, :], xnT[:, k, :], shift[:, k:k + 1], None, ALU.add)
                    ins.then_inc(sem("xn"), 1)
                ct.step("xn", KD)

            def add_to_h(src, wait):
                for k in range(KD):
                    wait(k)
                    V.tensor_tensor(hT[:, k, :], hT[:, k, :], src[:, k, :], ALU.add).then_inc(sem("h_ready"), 1)
                dve.wait_ge(sem("h_ready"), ct.step("h", KD))

            def scale_normed(src, gain):
                return [link(V.scalar_tensor_tensor(out=src[:, k, :], in0=src[:, k, :], scalar=gain[:, k:k + 1], in1=rinv[:, :],
                                                    op0=ALU.mult, op1=ALU.mult), wait=False) for k in range(KD)]

            def residual(src, gain):
                invert()
                marks = scale_normed(src, gain)
                add_to_h(src, lambda k: dve.wait_ge(link.sem, marks[k]))

            def copy_tiles(dst, chunks_per_tile):
                for k in range(KD):
                    n = take_tile(chunks_per_tile)
                    dve.wait_ge(sem("squares"), ct.step("squares"))
                    free_bank(V.tensor_copy(dst[:, k, :], bank_of(n)[:, :]), n)

            def log1p_of(u, out_, a, b):
                link(V.tensor_scalar(a, u, 2.0, None, ALU.add))
                link(V.reciprocal(a, a))
                link(V.tensor_tensor(out_, u, a, ALU.mult))
                link(V.tensor_tensor(a, out_, out_, ALU.mult))
                link(V.tensor_scalar(b, a, LOG1P_TERMS[-1], None, ALU.mult))
                for c in LOG1P_TERMS[-2::-1]:
                    link(V.scalar_tensor_tensor(out=b, in0=b, scalar=c, in1=a, op0=ALU.add, op1=ALU.mult))
                link(V.scalar_tensor_tensor(out=out_, in0=b, scalar=1.0, in1=out_, op0=ALU.add, op1=ALU.mult))
                link(V.tensor_scalar(out_, out_, 2.0, None, ALU.mult))

            def attention(n_units, bias_of, write, between=None):
                base = ct.n.get("unit", 0)

                def largest(u):
                    dve.wait_ge(sem("att_scores"), base + u + 1)
                    n = (u % TT + 1) * P
                    nm = nmax[:, u % 4:u % 4 + 1]
                    s = banks[5 + u % 3][:, 0:n]
                    bias = bias_of(u)
                    if bias is not None:
                        if u >= 3:
                            dve.wait_ge(sem("att_exp"), base + u - 2)
                        V.tensor_tensor_reduce(pbuf[:, u % 3, 0:n], s, bias, -1.0, HUGE, ALU.add, ALU.min, nm).then_inc(sem("att_max"), 1)
                    else:
                        if u >= 4:
                            dve.wait_ge(sem("att_exp"), base + u - 3)
                        V.tensor_reduce(nm, s, AX, ALU.max, negate=True).then_inc(sem("att_max"), 1)

                def copy(u):
                    dve.wait_ge(sem("att_turned"), base + u + 1)
                    if u >= 2:
                        dve.wait_ge(sem("att_values"), base + u - 1)
                    n = (u % TT + 1) * P
                    V.tensor_copy(ptb[:, u % 2, 0:n], banks[u % 2][:, 0:n]).then_inc(sem("att_copied0"), 1)

                def output(u):
                    dve.wait_ge(sem("att_values"), base + u + 1)
                    dve.wait_ge(sem("att_exp"), base + u + 1)
                    link(V.reciprocal(RCP[:, u % 4:u % 4 + 1], rsum[:, u % 4:u % 4 + 1]))
                    write(u, banks[2 + u % 2], RCP[:, u % 4:u % 4 + 1], base)

                for s in range(n_units + 3):
                    if s < n_units:
                        largest(s)
                    if s >= 2 and s % 2 == 0 and s - 2 < n_units:
                        copy(s - 2)
                    if s >= 3:
                        output(s - 3)
                    if between:
                        between(s)
                ct.n["unit"] = base + n_units

            V.memset(EPSC, EPS).then_inc(sem("eps"), 1)
            V.memset(SEPSC, SUBLN_EPS).then_inc(sem("eps"), 1)
            dve.wait_ge(sem("eps"), 2)
            dve.wait_ge(sem("lambda_loaded"), 16 * 6)
            link(V.tensor_tensor(small[:, 0:64], small[:, 0:64], small[:, 64:128], ALU.mult))
            link(V.tensor_tensor(small[:, 128:192], small[:, 128:192], small[:, 192:256], ALU.mult))
            link(V.tensor_reduce(LDOT[:, 0:1], small[:, 0:64], AX, ALU.add))
            V.tensor_reduce(LDOT[:, 1:2], small[:, 128:192], AX, ALU.add).then_inc(sem("lambda_dots"), 1)
            dve.wait_ge(sem("lambda_exp"), 1)
            link(V.tensor_tensor(NEGLAM, LEXP[:, 1:2], LEXP[:, 0:1], ALU.subtract))
            link(V.tensor_scalar(NEGLAM, NEGLAM, -LAM_INIT, None, ALU.add))
            n = take_turned()
            free_bank(V.tensor_copy(cols[:, :], bank_of(n)[:, 0:VTILES * P]), n)
            evacuated(dve, n)
            link(V.tensor_scalar(HBX, col("rec_bx", 0, KR), 0.5, None, ALU.mult))
            link(V.tensor_scalar(HBA, col("rec_ba", 0, KR), 0.5, None, ALU.mult))
            V.scalar_tensor_tensor(out=LPT[0][:, 0:KR], in0=col("rec_a_param", 0, KR), scalar=-1.0, in1=col("rec_a_param", 0, KR),
                                   op0=ALU.mult, op1=ALU.max).then_inc(sem("a_param_in"), 1)
            dve.wait_ge(sem("a_param_exp"), 1)
            log1p_of(LPT[1][:, 0:KR], LPT[2][:, 0:KR], LPT[3][:, 0:KR], LPT[4][:, 0:KR])
            link(V.tensor_scalar(LPT[0][:, 0:KR], col("rec_a_param", 0, KR), 0.0, None, ALU.min))
            link(V.tensor_tensor(LPT[0][:, 0:KR], LPT[0][:, 0:KR], LPT[2][:, 0:KR], ALU.subtract))
            link(V.tensor_scalar(C4, LPT[0][:, 0:KR], 4.0, None, ALU.mult))
            V.tensor_scalar(NC4, LPT[0][:, 0:KR], -4.0, None, ALU.mult).then_inc(sem("c4_ready"), 1)
            for k in range(KD):
                n = take_turned()
                free_bank(V.tensor_copy(hT[:, k, :], bank_of(n)[:, :]), n)
            for k in range(KD):
                evacuated(dve, 1 + k)
            ct.step("squares", KD)
            apply_norm(col("ln_mix_pre", 0, KD))

            for j, n0 in enumerate(QKV0):
                n = take_tile(1)
                bank = bank_of(n)
                if n0 == A_FZ:
                    free_bank(V.tensor_scalar(FZ[0], bank[0:8, :], small[0:8, 384:385], None, ALU.add), n)
                    evacuated(dve, n)
                    V.scalar_tensor_tensor(out=FZ[1], in0=FZ[0], scalar=-1.0, in1=FZ[0], op0=ALU.mult, op1=ALU.max).then_inc(sem("forget_in"), 1)
                elif j <= 8:
                    free_bank(V.tensor_scalar(big[:, j - 1, :], bank[:, :], HD ** -0.5, None, ALU.mult), n)
                elif j < NQK:
                    free_bank(V.tensor_copy(big[:, j - 1, :], bank[:, :]), n)
                else:
                    free_bank(V.tensor_copy(mT[:, j - NQK, :], bank[:, :]), n)
                if j == 3:
                    dve.wait_ge(sem("forget_exp"), 1)
                    log1p_of(FZ[2], FZ[1], FZ[3], FZ[4])
                    link(V.tensor_scalar(FZ[0], FZ[0], 0.0, None, ALU.min))
                    link(V.tensor_tensor(FZ[0], FZ[0], FZ[1], ALU.subtract))
                    link(V.memset(FZ[1], 1.0))
                    V.tensor_tensor_scan(CUM, FZ[1], FZ[0], 0.0, ALU.mult, ALU.add).then_inc(sem("log_forget"), 1)
            for j in range(8):
                n = take_turned()
                free_bank(V.tensor_copy(V0[:, :, j // 4, (j % 4) * P:(j % 4 + 1) * P], bank_of(n)[:, :].rearrange("p (a n) -> p a n", a=TT)), n)
            for h in range(8):
                n = take_turned()
                free_bank(V.tensor_copy(FB[:, h, :], bank_of(n)[:, :]), n)
                evacuated(dve, n)
            dve.wait_ge(sem("alibi"), 4)

            def bias0(u):
                m, n = u // TT, (u % TT + 1) * P
                return ALIBI[:, m // 2, T - n:T] if m < 8 else FB[:, m - 8, 0:n]

            def write0(u, bank, rcp, base):
                m, qi = u // TT, u % TT
                if m >= 8:
                    o = OTOK[:, qi, 512 + (m - 8) * HD:512 + (m - 7) * HD]
                    V.tensor_scalar(o, bank[:, 0:HD], rcp, None, ALU.mult).then_inc(sem("att_out"), 1)
                elif m % 2 == 0:
                    V.tensor_scalar(OTOK[:, qi, (m // 2) * P:(m // 2 + 1) * P], bank[:, 0:P], rcp, None, ALU.mult).then_inc(sem("att_out"), 1)
                else:
                    V.tensor_scalar(ot[:, 0:P], bank[:, 0:P], rcp, NEGLAM, ALU.mult, ALU.mult).then_inc(sem("att_out"), 1)
                    dve.wait_ge(sem("att_out"), base + u + 1)
                    o = OTOK[:, qi, (m // 2) * P:(m // 2 + 1) * P]
                    link(V.tensor_tensor(o, o, ot[:, 0:P], ALU.add))
            attention(64, bias0, write0)
            dve.wait_ge(sem("att_out"), 64)
            for qi in range(TT):
                link(V.tensor_tensor(pbuf[:, 0, :], OTOK[:, qi, 0:512], OTOK[:, qi, 0:512], ALU.mult))
                ins = V.tensor_reduce(SS[:, 4 * qi:4 * qi + 4], pbuf[:, 0, :].rearrange("p (h n) -> p h n", h=4), AX, ALU.add)
                if qi < TT - 1:
                    link(ins)
                else:
                    ins.then_inc(sem("subln_sums"), 1)
            dve.wait_ge(sem("subln_root"), 1)
            link(V.reciprocal(SS, SS))
            link(V.tensor_scalar(SS, SS, 1.0 - LAM_INIT, None, ALU.mult))
            for qi in range(TT):
                o = OTOK[:, qi, 0:512].rearrange("p (h n) -> p h n", h=4)
                link(V.tensor_tensor(o, o, SS[:, 4 * qi:4 * qi + 4].unsqueeze(2).broadcast_to([P, 4, P]), ALU.mult))
                V.tensor_tensor(o, o, small[:, 256:384].unsqueeze(1).broadcast_to([P, 4, P]), ALU.mult).then_inc(sem("subln_done"), 1)
            for k in range(KD):
                n = take_turned()
                free_bank(V.tensor_copy(xnT[:, k, :], bank_of(n)[:, :]), n)
            copy_tiles(mT, 1)
            for k in range(KD):
                evacuated(dve, ct.tile - KD + k)
            residual(mT, col("ln_mix_post", 0, KD))

            for layer in range(2):
                if layer == 1:
                    ct.step("squares", KD)
                    apply_norm(col("ln_mix_pre", KD, KD))
                    link(V.memset(CIN[:, :, 0:3], 0.0))
                    for i in range(KR):
                        n = take_tile(1)
                        x = CIN[:, i % 2, :]
                        free_bank(V.tensor_copy(x[:, 3:3 + T], bank_of(n)[:, :]), n)
                        evacuated(dve, n)
                        link(V.tensor_scalar(big[:, i, :], x[:, 3:3 + T], col("rec_conv_w", 3 * KR + i), col("rec_conv_b", i), ALU.mult, ALU.add))
                        for j in (2, 1, 0):
                            ins = V.scalar_tensor_tensor(out=big[:, i, :], in0=x[:, j:j + T], scalar=col("rec_conv_w", j * KR + i),
                                                         in1=big[:, i, :], op0=ALU.mult, op1=ALU.add)
                            if j:
                                link(ins)
                            else:
                                ins.then_inc(sem("conv_out"), 1)
                    dve.wait_ge(sem("conv_out"), KR)
                    ct.chunk, ct.tile = ct.chunk + KR, ct.tile + KR
                    for i in range(KR):
                        evacuated(dve, ct.tile)
                        dve.wait_ge(turned, ct.n["turned"] + 2)
                        V.scalar_tensor_tensor(out=big[:, i, :], in0=tmpA[:, i % 2, :], scalar=1.0, in1=big[:, i, :],
                                               op0=ALU.add, op1=ALU.mult).then_inc(sem("gate_x_used"), 1)
                        dve.wait_ge(sem("gate_a_read"), 2 * (i + 1))
                        link(V.tensor_tensor(tmpD[:, i % 2, :], big[:, 20 + i, :], big[:, 20 + i, :], ALU.mult))
                        V.scalar_tensor_tensor(out=big[:, 30 + i, :], in0=tmpD[:, i % 2, :], scalar=1.0, in1=big[:, 30 + i, :],
                                               op0=ALU.add, op1=ALU.mult).then_inc(sem("one_minus_a2"), 1)
                        ct.step("turned", 2)
                        ct.tile += 2
                    dve.wait_ge(sem("gate_x_used"), KR)
                    for i in range(KR):
                        dve.wait_ge(sem("mult_ready"), i + 1)
                        link(V.memset(big[:, 30 + i, 0:1], 1.0))
                        link(V.scalar_tensor_tensor(out=big[:, i, :], in0=big[:, 30 + i, :], scalar=0.5, in1=big[:, i, :],
                                                    op0=ALU.mult, op1=ALU.mult))
                        link(V.tensor_tensor_scan(big[:, 30 + i, :], big[:, 20 + i, :], big[:, i, :], 0.0, ALU.mult, ALU.add))
                        V.tensor_tensor(big[:, i, :], big[:, 30 + i, :], big[:, 10 + i, :], ALU.mult).then_inc(sem("rec_out"), 1)
                    copy_tiles(mT, 2)
                    for k in range(KD):
                        evacuated(dve, ct.tile - KD + k)
                    residual(mT, col("ln_mix_post", KD, KD))
                ct.step("squares", KD)
                apply_norm(col("ln_mlp_pre", KD * layer, KD))
                c0, t0 = ct.chunk, ct.tile
                with dve.Fori(0, 4) as i:
                    for j in range(8):
                        dve.wait_ge(chunk_used, c0 + j + 1 + i * 8)
                        free_bank(V.tensor_scalar(tmpD[:, j % 2, :], bank_of(t0 + j)[:, :], 0.0, None, ALU.max), t0 + j)
                        dve.wait_ge(bank_free[(t0 + j) % NB], (t0 + j) // NB + 1 + i * 2)
                        V.tensor_tensor(big[:, bass.ds(i * 8 + j, 1), :], tmpD[:, j % 2, :], tmpD[:, j % 2, :], ALU.mult).then_inc(sem("hidden"), 1)
                c0, t0 = c0 + 32, t0 + 32
                s0 = ct.n["squares"]
                with dve.Fori(0, 2) as i:
                    for j in range(4):
                        dve.wait_ge(sem("squares"), s0 + j + 1 + i * 4)
                        free_bank(V.tensor_copy(mT[:, bass.ds(i * 4 + j, 1), :], bank_of(t0 + j)[:, :]), t0 + j)
                ct.step("squares", KD)
                ct.chunk, ct.tile = c0 + 32, t0 + 8
                for k in range(KD):
                    evacuated(dve, ct.tile - KD + k)
                residual(mT, col("ln_mlp_post", KD * layer, KD))
                for k in range(2):
                    n = take_turned()
                    free_bank(V.tensor_copy(big[:, 18 + k, :], bank_of(n)[:, :]), n)
                copy_tiles(arena(0, KD), 1)
                for k in range(KD):
                    evacuated(dve, ct.tile - KD + k)
                invert()
                marks = scale_normed(arena(0, KD), col("ple_norm", KD * layer, KD))
                dve.wait_ge(link.sem, marks[-1])
                for k in range(KD):
                    ct.chunk, ct.tile = ct.chunk + 1, ct.tile + 1
                    evacuated(dve, ct.tile - 1)
                    V.tensor_tensor(big[:, k, :], big[:, k, :], tmpA[:, k % 2, :], ALU.mult).then_inc(sem("gated"), 1)
                    ct.step("gated")
                dve.wait_ge(chunk_used, ct.chunk)
                add_to_h(arena(0, KD), lambda k: dve.wait_ge(sem("gated"), ct.n["gated"] - KD + k + 1))
                if STOP == f"layer{layer}":
                    break
            if STOP == "all":
                dve2(dve, ct, link, take_tile, take_turned, invert, apply_norm, add_to_h, copy_tiles, attention)


_INS = ["x", "p", "ln_mix_pre", "ln_mix_post", "ln_mlp_pre", "ln_mlp_post", "mlp_w_up", "mlp_w_down", "ple_w_proj",
        "ple_norm", "ple_w_gate", "attn_w_in", "attn_b_forget", "attn_w_out", "diff_lambda_q1", "diff_lambda_k1",
        "diff_lambda_q2", "diff_lambda_k2", "diff_subln", "rec_w_in", "rec_conv_w", "rec_conv_b", "rec_wx",
        "rec_bx", "rec_wa", "rec_ba", "rec_a_param", "rec_w_out", "c_2", "ada_w_2", "ada_b_2", "norm1_g_2", "w_in_2",
        "ssm_lam_re_2", "ssm_lam_im_2", "ssm_log_dt_2", "ssm_b_re_2", "ssm_b_im_2", "ssm_c_re_2", "ssm_c_im_2",
        "ssm_d_2", "ssm_w_glu_2", "ssm_w_o_2", "nsa_cmp_pos_2", "nsa_cmp_w1_2", "nsa_cmp_w2_2", "nsa_w_o_2",
        "w_out_2", "norm2_g_2", "moe_w_group_2", "moe_b_group_2", "moe_w_expert_2", "moe_b_expert_2",
        "moe_w_gate_2", "moe_w_up_2", "moe_w_down_2", "final_g_2"]
_OUT = (1, T, D)


def kernel(**inputs):
    import numpy as np
    import concourse.bacc as bacc
    from concourse.bass_utils import run_bass_kernel_spmd

    nc = bacc.Bacc("TRN2", target_bir_lowering=False, num_devices=1)
    arrays, aps = {}, {}
    for name in _INS:
        a = np.ascontiguousarray(inputs[name])
        arrays[f"in_{name}_dram"] = a
        aps[name] = nc.dram_tensor(f"in_{name}_dram", a.shape, mybir.dt.from_np(a.dtype), kind="ExternalInput").ap()
    out = nc.dram_tensor("out_0_dram", _OUT, F32, kind="ExternalOutput").ap()
    model_kernel(nc, aps, out)
    r = run_bass_kernel_spmd(nc, [arrays], core_ids=[0])
    return r.results[0]["out_0_dram"]
```
